# Optimizing a Trainium2 kernel written in Bass

```python
import math
import jax, jax.numpy as jnp
from jax import lax
import numpy as np

D_MODEL = 1024
BATCH = 1
SEQ = 512
DEPTH = 1
DEC_BATCH = 8
DEC_SEQ = 4
PAST_LEN = 256
PAGE_SIZE = 128

GDN_HEADS = 8
GDN_HEAD_DIM = 64
GDN_WIDTH = GDN_HEADS * GDN_HEAD_DIM
CONV_WIDTH = 4
CONV_DIM = 3 * GDN_WIDTH
GDN_CHUNK = 64
FOX_HEADS = 8
FOX_HEAD_DIM = 64
FOX_WIDTH = FOX_HEADS * FOX_HEAD_DIM
Q_BLOCK = 128
N_EXPERTS = 64
N_GROUPS = 8
TOPK_GROUPS = 4
TOP_K = 8
EXPERT_FF = 256
SHARED_FF = 256
ROUTED_SCALE = 2.5
DEEPNORM_ALPHA = (2.0 * DEPTH) ** 0.25
DEEPNORM_BETA = (8.0 * DEPTH) ** -0.25
LN_EPS = 1e-5
RMS_EPS = 1e-6
IN_SIZES = (CONV_DIM, GDN_WIDTH, GDN_HEADS, GDN_HEADS, FOX_WIDTH, FOX_WIDTH, FOX_WIDTH, FOX_HEADS, D_MODEL, D_MODEL)
N_IN = sum(IN_SIZES)

kernel_name = 'hybrid_gdn_fox_moe_deepnorm_adaln_step'

def _split_cols(t, sizes):
    cuts, acc = [], 0
    for s in sizes[:-1]:
        acc += s
        cuts.append(acc)
    return jnp.split(t, cuts, axis=-1)

def _layernorm(x, g, b):
    xf = x.astype(jnp.float32)
    xc = xf - jnp.mean(xf, -1, keepdims=True)
    var = jnp.mean(xc * xc, -1, keepdims=True)
    return (xc * lax.rsqrt(var + LN_EPS) * g + b).astype(x.dtype)

def _rmsnorm(x, g):
    return x * lax.rsqrt(jnp.mean(x * x, -1, keepdims=True) + RMS_EPS) * g

def _l2norm(x):
    return x * lax.rsqrt(jnp.sum(x * x, -1, keepdims=True) + RMS_EPS)

def _causal_conv(x, buf, w):
    n = x.shape[1]
    xp = jnp.concatenate([buf.astype(x.dtype), x], axis=1)
    out = xp[:, 0:n] * w[0]
    for i in range(1, CONV_WIDTH):
        out = out + xp[:, i:i + n] * w[i]
    return jax.nn.silu(out), xp[:, n:]

def _to_chunks(t, n_chunks, c):
    t = t.reshape((t.shape[0], n_chunks, c) + t.shape[2:])
    return jnp.swapaxes(jnp.moveaxis(t, 1, 0), 2, 3)

def _gdn_chunked(q, k, v, beta, g, s0, chunk):
    nb, n, nh, dk = q.shape
    dv = v.shape[-1]
    nc = n // chunk
    q, k, v = _to_chunks(q, nc, chunk), _to_chunks(k, nc, chunk), _to_chunks(v, nc, chunk)
    beta, g = _to_chunks(beta, nc, chunk), _to_chunks(g, nc, chunk)
    big_g = jnp.cumsum(g, axis=-1)
    idx = jnp.arange(chunk)
    incl = idx[:, None] >= idx[None, :]
    strict = idx[:, None] > idx[None, :]
    gdiff = big_g[..., :, None] - big_g[..., None, :]
    dec_incl = jnp.exp(jnp.where(incl, gdiff, -jnp.inf))
    dec_strict = jnp.where(strict, dec_incl, 0.0)
    lmat = beta[..., :, None] * jnp.einsum('nbhik,nbhjk->nbhij', k, k) * dec_strict
    gam = jnp.exp(big_g)
    rhs = beta[..., None] * jnp.concatenate([v, gam[..., None] * k], axis=-1)
    sol = lax.linalg.triangular_solve(lmat, rhs, left_side=True, lower=True, unit_diagonal=True)
    w1, w2 = sol[..., :dv], sol[..., dv:]
    aqk = jnp.einsum('nbhik,nbhjk->nbhij', q, k) * dec_incl
    qg = gam[..., None] * q
    kd = jnp.exp(big_g[..., -1:] - big_g)[..., None] * k
    glast = gam[..., -1]

    def step(s, xs):
        w1c, w2c, qgc, aqkc, kdc, glc = xs
        u = w1c - jnp.einsum('bhck,bhkv->bhcv', w2c, s)
        o = jnp.einsum('bhck,bhkv->bhcv', qgc, s) + jnp.einsum('bhij,bhjv->bhiv', aqkc, u)
        s = glc[..., None, None] * s + jnp.einsum('bhck,bhcv->bhkv', kdc, u)
        return s, o

    s_fin, o = lax.scan(step, s0, (w1, w2, qg, aqk, kd, glast))
    o = jnp.moveaxis(jnp.swapaxes(o, 2, 3), 0, 1).reshape(nb, n, nh, dv)
    return o, s_fin

def _fox_prompt(q, k, v, logf):
    nb, n, nh, hd = q.shape
    scale = hd ** -0.5
    big_f = jnp.cumsum(logf, axis=1)
    nblk = n // Q_BLOCK
    qb = jnp.swapaxes(q.reshape(nb, nblk, Q_BLOCK, nh, hd), 0, 1)
    fb = jnp.swapaxes(big_f.reshape(nb, nblk, Q_BLOCK, nh), 0, 1)
    pos = jnp.arange(n)
    posb = pos.reshape(nblk, Q_BLOCK)
    fk = jnp.transpose(big_f, (0, 2, 1))[:, :, None, :]

    def one_block(args):
        qc, fc, pc = args
        s = jnp.einsum('bqhd,bkhd->bhqk', qc, k) * scale + jnp.transpose(fc, (0, 2, 1))[..., None] - fk
        s = jnp.where(pc[:, None] >= pos[None, :], s, -jnp.inf)
        p = jax.nn.softmax(s, axis=-1)
        return jnp.einsum('bhqk,bkhd->bqhd', p, v)

    o = lax.map(one_block, (qb, fb, posb))
    return jnp.swapaxes(o, 0, 1).reshape(nb, n, nh, hd)

def _fox_sample(q, k, v, logf, k_past, v_past, logf_past):
    hd = q.shape[-1]
    n = q.shape[1]
    scale = hd ** -0.5
    k_past = k_past.astype(jnp.float32)
    v_past = v_past.astype(jnp.float32)
    lfp = logf_past.astype(jnp.float32)
    suffix = lax.cumsum(lfp, axis=1, reverse=True) - lfp
    fn = jnp.transpose(jnp.cumsum(logf, axis=1), (0, 2, 1))
    s_past = (jnp.einsum('blhd,bphd->bhlp', q, k_past) * scale + fn[..., None]
              + jnp.transpose(suffix, (0, 2, 1))[:, :, None, :])
    idx = jnp.arange(n)
    s_new = jnp.einsum('blhd,bmhd->bhlm', q, k) * scale + fn[..., :, None] - fn[..., None, :]
    s_new = jnp.where(idx[:, None] >= idx[None, :], s_new, -jnp.inf)
    p = jax.nn.softmax(jnp.concatenate([s_past, s_new], axis=-1), axis=-1)
    npast = k_past.shape[1]
    return (jnp.einsum('bhlp,bphd->blhd', p[..., :npast], v_past)
            + jnp.einsum('bhlm,bmhd->blhd', p[..., npast:], v))

def _moe(h, w_router, router_bias, w_gate, w_up, w_down, ws_gate, ws_up, ws_down):
    shp = h.shape
    x = h.reshape(-1, shp[-1])
    n_tok = x.shape[0]
    s = jax.nn.sigmoid((x @ w_router).astype(jnp.float32))
    sb = s + router_bias.astype(jnp.float32)
    grp = sb.reshape(n_tok, N_GROUPS, N_EXPERTS // N_GROUPS)
    gscore = jnp.sum(lax.top_k(grp, 2)[0], axis=-1)
    _, gidx = lax.top_k(gscore, TOPK_GROUPS)
    gmask = jnp.sum(jax.nn.one_hot(gidx, N_GROUPS), axis=1) > 0
    emask = jnp.repeat(gmask, N_EXPERTS // N_GROUPS, axis=1)
    _, eidx = lax.top_k(jnp.where(emask, sb, -jnp.inf), TOP_K)
    wsel = jnp.take_along_axis(s, eidx, axis=1)
    wsel = wsel / jnp.sum(wsel, axis=-1, keepdims=True) * ROUTED_SCALE
    gates = jnp.einsum('tk,tke->te', wsel, jax.nn.one_hot(eidx, N_EXPERTS, dtype=wsel.dtype))

    def expert(acc, xs):
        wg, wu, wd, ge = xs
        y = (jax.nn.silu(x @ wg) * (x @ wu)) @ wd
        return acc + ge[:, None] * y.astype(jnp.float32), None

    routed, _ = lax.scan(expert, jnp.zeros((n_tok, shp[-1]), jnp.float32), (w_gate, w_up, w_down, gates.T))
    shared = (jax.nn.silu(x @ ws_gate) * (x @ ws_up)) @ ws_down
    return (routed + shared.astype(jnp.float32)).reshape(shp).astype(h.dtype)

def _layer(x, c, p, conv_buf, ssm0, fox_past):
    (w_ada, b_ada, w_in, conv_w, a_log, dt_bias, norm_g, f_bias, w_ba, w_bb, w_out, ln1_g, ln1_b,
     w_router, router_bias, w_gate, w_up, w_down, ws_gate, ws_up, ws_down, ln2_g, ln2_b) = p
    f32 = jnp.float32
    nb, n, _ = x.shape
    mod = (c @ w_ada + b_ada)[:, None, :]
    sh1, sc1, gt1, sh2, sc2, gt2 = jnp.split(mod, 6, axis=-1)
    h = x * (1.0 + sc1) + sh1
    (qkv_a, z_a, b_a, a_a, q_b, k_b, v_b, f_b, g_a, g_b) = _split_cols(h @ w_in, IN_SIZES)
    qkv_a, conv_new = _causal_conv(qkv_a, conv_buf, conv_w)
    q_a, k_a, v_a = jnp.split(qkv_a.astype(f32), 3, axis=-1)
    hs = (nb, n, GDN_HEADS, GDN_HEAD_DIM)
    q_a = _l2norm(q_a.reshape(hs)) * GDN_HEAD_DIM ** -0.5
    k_a = _l2norm(k_a.reshape(hs))
    v_a = v_a.reshape(hs)
    beta = jax.nn.sigmoid(b_a.astype(f32))
    g = -jnp.exp(a_log.astype(f32)) * jax.nn.softplus(a_a.astype(f32) + dt_bias.astype(f32))
    chunk = GDN_CHUNK if n % GDN_CHUNK == 0 else n
    o_a, ssm_new = _gdn_chunked(q_a, k_a, v_a, beta, g, ssm0.astype(f32), chunk)
    o_a = _rmsnorm(o_a, norm_g.astype(f32)) * jax.nn.silu(z_a.astype(f32).reshape(hs))
    o_a = o_a.reshape(nb, n, GDN_WIDTH).astype(x.dtype)
    fs = (nb, n, FOX_HEADS, FOX_HEAD_DIM)
    logf = jax.nn.log_sigmoid(f_b.astype(f32) + f_bias.astype(f32))
    q_b = q_b.astype(f32).reshape(fs)
    k_b = k_b.astype(f32).reshape(fs)
    v_b = v_b.astype(f32).reshape(fs)
    if fox_past is None:
        o_b = _fox_prompt(q_b, k_b, v_b, logf)
    else:
        o_b = _fox_sample(q_b, k_b, v_b, logf, fox_past[0], fox_past[1], fox_past[2])
    o_b = o_b.reshape(nb, n, FOX_WIDTH).astype(x.dtype)
    merged = jax.nn.sigmoid(g_a) * (o_a @ w_ba) + jax.nn.sigmoid(g_b) * (o_b @ w_bb)
    x = _layernorm(DEEPNORM_ALPHA * x + gt1 * (merged @ w_out), ln1_g, ln1_b)
    h2 = x * (1.0 + sc2) + sh2
    ffn = _moe(h2, w_router, router_bias, w_gate, w_up, w_down, ws_gate, ws_up, ws_down)
    x = _layernorm(DEEPNORM_ALPHA * x + gt2 * ffn, ln2_g, ln2_b)
    return x, (k_b.astype(x.dtype), v_b.astype(x.dtype), logf.astype(x.dtype), ssm_new, conv_new)

def setup_inputs(seed: int = 0) -> dict:
    key = jax.random.key(seed)
    ks = iter(jax.random.split(key, 40))
    f32 = jnp.float32

    def nrm(shape, scale=1.0):
        return jax.random.normal(next(ks), shape, f32) * scale

    n_pages = PAST_LEN // PAGE_SIZE
    n_used = DEC_BATCH * n_pages
    n_phys = n_used + max(n_used // 4, 1)
    x_prompt = nrm((BATCH, SEQ, D_MODEL))
    x_sample = nrm((DEC_BATCH, DEC_SEQ, D_MODEL))
    c_prompt = nrm((BATCH, D_MODEL))
    c_sample = nrm((DEC_BATCH, D_MODEL))
    cache_k = nrm((DEPTH, n_phys, PAGE_SIZE, FOX_HEADS, FOX_HEAD_DIM))
    cache_v = nrm((DEPTH, n_phys, PAGE_SIZE, FOX_HEADS, FOX_HEAD_DIM))
    cache_logf = jax.nn.log_sigmoid(nrm((DEPTH, n_phys, PAGE_SIZE, FOX_HEADS)) + 8.0)
    state_ssm = nrm((DEPTH, DEC_BATCH, GDN_HEADS, GDN_HEAD_DIM, GDN_HEAD_DIM), 0.3)
    state_conv = nrm((DEPTH, DEC_BATCH, CONV_WIDTH - 1, CONV_DIM))
    page_table = jax.random.permutation(next(ks), n_phys)[:n_used].reshape(DEC_BATCH, n_pages).astype(jnp.int32)
    d = D_MODEL
    w_ada = nrm((DEPTH, d, 6 * d), 0.5 * d ** -0.5)
    b_ada = nrm((DEPTH, 6 * d), 0.02)
    w_in = nrm((DEPTH, d, N_IN), d ** -0.5)
    conv_w = nrm((DEPTH, CONV_WIDTH, CONV_DIM), CONV_WIDTH ** -0.5)
    gdn_a_log = jnp.log(jax.random.uniform(next(ks), (DEPTH, GDN_HEADS), f32, 1.0, 16.0))
    dt = jnp.exp(jax.random.uniform(next(ks), (DEPTH, GDN_HEADS), f32, math.log(1e-3), math.log(1e-1)))
    gdn_dt_bias = dt + jnp.log(-jnp.expm1(-dt))
    gdn_norm_g = 1.0 + nrm((DEPTH, GDN_HEAD_DIM), 0.02)
    fox_f_bias = jax.random.uniform(next(ks), (DEPTH, FOX_HEADS), f32, 1.0, 4.0)
    w_branch_a = nrm((DEPTH, GDN_WIDTH, d), GDN_WIDTH ** -0.5 * DEEPNORM_BETA)
    w_branch_b = nrm((DEPTH, FOX_WIDTH, d), FOX_WIDTH ** -0.5 * DEEPNORM_BETA)
    w_out = nrm((DEPTH, d, d), d ** -0.5 * DEEPNORM_BETA)
    ln1_g = 1.0 + nrm((DEPTH, d), 0.02)
    ln1_b = nrm((DEPTH, d), 0.02)
    w_router = nrm((DEPTH, d, N_EXPERTS), d ** -0.5)
    router_bias = nrm((DEPTH, N_EXPERTS), 0.01)
    w_gate = nrm((DEPTH, N_EXPERTS, d, EXPERT_FF), d ** -0.5)
    w_up = nrm((DEPTH, N_EXPERTS, d, EXPERT_FF), d ** -0.5)
    w_down = nrm((DEPTH, N_EXPERTS, EXPERT_FF, d), EXPERT_FF ** -0.5 * DEEPNORM_BETA)
    ws_gate = nrm((DEPTH, d, SHARED_FF), d ** -0.5)
    ws_up = nrm((DEPTH, d, SHARED_FF), d ** -0.5)
    ws_down = nrm((DEPTH, SHARED_FF, d), SHARED_FF ** -0.5 * DEEPNORM_BETA)
    ln2_g = 1.0 + nrm((DEPTH, d), 0.02)
    ln2_b = nrm((DEPTH, d), 0.02)
    return dict(x_prompt=x_prompt, x_sample=x_sample, c_prompt=c_prompt, c_sample=c_sample,
                cache_k=cache_k, cache_v=cache_v, cache_logf=cache_logf, state_ssm=state_ssm,
                state_conv=state_conv, page_table=page_table, w_ada=w_ada, b_ada=b_ada, w_in=w_in,
                conv_w=conv_w, gdn_a_log=gdn_a_log, gdn_dt_bias=gdn_dt_bias, gdn_norm_g=gdn_norm_g,
                fox_f_bias=fox_f_bias, w_branch_a=w_branch_a, w_branch_b=w_branch_b, w_out=w_out,
                ln1_g=ln1_g, ln1_b=ln1_b, w_router=w_router, router_bias=router_bias, w_gate=w_gate,
                w_up=w_up, w_down=w_down, ws_gate=ws_gate, ws_up=ws_up, ws_down=ws_down,
                ln2_g=ln2_g, ln2_b=ln2_b)

def reference(x_prompt, x_sample, c_prompt, c_sample, cache_k, cache_v, cache_logf, state_ssm,
              state_conv, page_table, w_ada, b_ada, w_in, conv_w, gdn_a_log, gdn_dt_bias, gdn_norm_g,
              fox_f_bias, w_branch_a, w_branch_b, w_out, ln1_g, ln1_b, w_router, router_bias, w_gate,
              w_up, w_down, ws_gate, ws_up, ws_down, ln2_g, ln2_b):
    n_seq, n_pages = page_table.shape
    past = n_pages * cache_k.shape[2]
    bp = x_prompt.shape[0]
    yp, ys = x_prompt, x_sample
    kp_l, vp_l, fp_l, sp_l, cp_l = [], [], [], [], []
    ks_l, vs_l, fs_l, ss_l, cs_l = [], [], [], [], []
    for l in range(DEPTH):
        p = (w_ada[l], b_ada[l], w_in[l], conv_w[l], gdn_a_log[l], gdn_dt_bias[l], gdn_norm_g[l],
             fox_f_bias[l], w_branch_a[l], w_branch_b[l], w_out[l], ln1_g[l], ln1_b[l], w_router[l],
             router_bias[l], w_gate[l], w_up[l], w_down[l], ws_gate[l], ws_up[l], ws_down[l],
             ln2_g[l], ln2_b[l])
        conv0 = jnp.zeros((bp, CONV_WIDTH - 1, CONV_DIM), yp.dtype)
        ssm0 = jnp.zeros((bp, GDN_HEADS, GDN_HEAD_DIM, GDN_HEAD_DIM), jnp.float32)
        yp, (kp, vp, fp, sp, cp) = _layer(yp, c_prompt, p, conv0, ssm0, None)
        k_past = jnp.take(cache_k[l], page_table, axis=0).reshape(n_seq, past, FOX_HEADS, FOX_HEAD_DIM)
        v_past = jnp.take(cache_v[l], page_table, axis=0).reshape(n_seq, past, FOX_HEADS, FOX_HEAD_DIM)
        f_past = jnp.take(cache_logf[l], page_table, axis=0).reshape(n_seq, past, FOX_HEADS)
        ys, (k_s, v_s, f_s, s_s, c_s) = _layer(ys, c_sample, p, state_conv[l], state_ssm[l],
                                               (k_past, v_past, f_past))
        kp_l.append(kp); vp_l.append(vp); fp_l.append(fp); sp_l.append(sp); cp_l.append(cp)
        ks_l.append(k_s); vs_l.append(v_s); fs_l.append(f_s); ss_l.append(s_s); cs_l.append(c_s)
    return (yp, ys, jnp.stack(kp_l), jnp.stack(vp_l), jnp.stack(fp_l), jnp.stack(sp_l), jnp.stack(cp_l),
            jnp.stack(ks_l), jnp.stack(vs_l), jnp.stack(fs_l), jnp.stack(ss_l), jnp.stack(cs_l))


_drawn_inputs = setup_inputs


def setup_inputs(seed=0):
    import zlib

    import numpy as np

    out = dict(_drawn_inputs(seed))
    spreads = {}
    factors = {'cache_k': 3.47,
     'cache_logf': 36.224,
     'gdn_norm_g': 12.849,
     'ln2_g': 8.322,
     'ln2_b': 7.915}
    for name, (base, spread) in spreads.items():
        noise = np.random.default_rng([zlib.crc32(name.encode()), seed]).standard_normal(out[name].shape)
        drawn = base * np.exp(spread * noise) if base else spread * noise
        out[name] = __import__('jax').numpy.asarray(drawn.astype(out[name].dtype))
    for name, factor in factors.items():
        out[name] = (out[name] * factor).astype(out[name].dtype)
    return out
```

```python
import numpy as np
import concourse.bass as bass
from concourse import mybir

F32 = mybir.dt.float32
I32 = mybir.dt.int32
U32 = mybir.dt.uint32
ALU = mybir.AluOpType
ACT = mybir.ActivationFunctionType
AX = mybir.AxisListType

P = 128
D = 1024
KD = D // P
SEQ = 512
DB, DS = 8, 4
NS_TOK = DB * DS
PT = SEQ // P
NT = PT + 1
TOK = SEQ + NS_TOK
HALF = TOK // 2
TOKS = [P] * PT + [NS_TOK]
H, HD = 8, 64
W = H * HD
CW = W // P
CONV, CT = 4, 3 * W // P
E, GRP, TOPG, TOPK = 64, 8, 4, 8
FF = 256
PAGE, NPG, NPHYS = 128, 2, 20
ALPHA = 2.0 ** 0.25
LN_EPS, RMS_EPS = 1e-5, 1e-6
SCALE = HD ** -0.5
ROUTED = 2.5
NEG = -1e30
SLOT = 4096
NRING = 3
COL = dict(qkv=0, z=3 * W, b=4 * W, a=4 * W + H, q=4 * W + 2 * H, k=5 * W + 2 * H, v=6 * W + 2 * H,
           f=7 * W + 2 * H, ga=7 * W + 3 * H, gb=7 * W + 3 * H + D)

RING = 4
OVER = 36
NU = E + OVER + 4
UW = 6144
DUMMY = P


class Tick:
    live = []

    def __init__(self, nc, name):
        self.sem, self.n = nc.alloc_semaphore(name), 0
        Tick.live.append(self)

    def inc(self, ins, by=1):
        ins.then_inc(self.sem, by)
        self.n += by
        return self.n


def chained(eng, tick):
    def run(ins):
        eng.wait_ge(tick.sem, tick.inc(ins))
    return run


def build(nc, A, O):
    Tick.live.clear()
    sb = nc.alloc_sbuf_tensor("arena", [P, 53200], F32)
    bank = [nc.alloc_psum_tensor(f"bank{i}", [P, 512], F32) for i in range(8)]

    def at(off, *dims, p=P, dt=None):
        size = int(np.prod(dims))
        v = sb[0:p, off:off + size]
        if dt is not None:
            v = v.bitcast(dt)
        if len(dims) > 1:
            names = "abcde"[:len(dims)]
            v = v.rearrange(f"p ({' '.join(names)}) -> p {' '.join(names)}",
                            **{n: d for n, d in zip(names, dims)})
        return v

    kept = []

    def next_phases():
        ended = [s for s in Tick.live if s not in kept]
        nc.clear_and_free_semaphores([s.sem for s in ended])
        Tick.live[:] = [s for s in Tick.live if s in kept]
        nc.all_engine_barrier()

    def done(tick, ins):
        nc.vector.wait_ge(tick.sem, tick.inc(ins))

    slot = [at(i * SLOT, SLOT) for i in range(NRING)]
    T1 = NRING * SLOT
    X0 = 24576
    x_tm = at(X0, NT, D)
    hT = at(X0 + 5120, KD, TOK)
    modb = at(X0 + 9472, 2 * D, p=DB + 1)
    oTb = at(X0 + 11520, CW, TOK)
    oTa = at(X0 + 13696, CW, TOK)
    c = X0 + 15872
    def const(*dims, p=P):
        nonlocal c
        v = at(c, *dims, p=p)
        c += int(np.prod(dims))
        return v
    ident, causneg, cumU, ones = const(P), const(P), const(P), const(P)
    chunk1, chunkU, decneg = const(P), const(P), const(P)
    strictL, strictU = const(P), const(P)
    lvl = const(6, P)
    E8 = const(H, P, p=H)
    selP, selS = const(P, p=DB + 1), const(NS_TOK, p=DB + 1)
    EH = const(NS_TOK, p=H)
    sampU = const(NS_TOK, p=NS_TOK)
    R = const(DS, p=NS_TOK)
    MB4, MB = const(H, DS, p=NS_TOK), const(H, p=NS_TOK)
    newneg = const(DB, DB * DS, p=NS_TOK)
    bias24, nega, normg = const(24), const(H), const(HD)
    sm, beta, gdec, logf = const(NT, 24), const(NT, H), const(NT, H), const(NT, H)
    nF = const(TOK, p=H)
    cT, w24 = const(KD, DB + 1), const(KD, 24)
    nm, rsum, rinv = const(PT * H), const(PT * H), const(PT * H)
    lfp = const(DB * NPG, H)
    T2 = c
    END = 53200

    w_in = A["w_in"][0].rearrange("(k p) n -> p k n", p=P)
    w_ada = A["w_ada"][0].rearrange("(k p) n -> p k n", p=P)
    def in_cols(a, n=512):
        return w_in[:, :, a:a + n], n
    def ada_cols(a, n=512):
        return w_ada[:, :, a:a + n], n
    wo_v = A["w_out"][0].rearrange("(k p) n -> p k n", p=P)
    stream = [ada_cols(512 * i) for i in range(4)]
    stream += [in_cols(COL["q"]), in_cols(COL["k"]), in_cols(COL["v"])]
    stream += [in_cols(512 * i) for i in range(3)] + [in_cols(COL["z"])]
    GATES = len(stream)
    for i in range(2):
        stream += [in_cols(COL["ga"] + 512 * i), in_cols(COL["gb"] + 512 * i)]
    OUTP = len(stream)
    stream += [ada_cols(2048), ada_cols(2560), (wo_v[:, :, 0:512], 512), (wo_v[:, :, 512:1024], 512)]
    stream += [ada_cols(3072 + 512 * i) for i in range(4)]
    stream += [ada_cols(5120), ada_cols(5632)]
    loaded = [Tick(nc, f"stream_loaded{i}") for i in range(NRING)]
    last_use = {}
    sent = [0]

    def send_until(sp, n):
        while sent[0] < min(n, len(stream)):
            i = sent[0]
            src, cols = stream[i]
            if i >= NRING:
                sp.wait_ge(*last_use[i - NRING])
            loaded[i % NRING].inc(sp.dma_start(slot[i % NRING][:, 0:KD * cols].rearrange(
                "p (k n) -> p k n", k=KD), src), 16)
            sent[0] += 1

    def arrived(pe, i):
        pe.wait_ge(loaded[i % NRING].sem, 16 * (i // NRING + 1))
        return slot[i % NRING].rearrange("p (k n) -> p k n", k=KD)

    def read_by(i, tick):
        last_use[i] = (tick.sem, tick.n)

    vch, ach, gch = Tick(nc, "vector_step"), Tick(nc, "scalar_step"), Tick(nc, "pool_step")
    stored = Tick(nc, "outputs_stored")
    kept += [*loaded, vch, ach, gch, stored]

    QB = at(T2, DB * CW * DS, H)

    call = at(T1, D, p=DB + 1)
    h_tm = [at(T1 + 1400 + i * D, D) for i in range(2)]
    cload, xload, small = Tick(nc, "c_loaded"), Tick(nc, "x_loaded"), Tick(nc, "small_loaded")
    cT_ready, cT_sb = Tick(nc, "cT_in_psum"), Tick(nc, "cT_copied")
    mod_mm, mod_sb = Tick(nc, "mod_product"), Tick(nc, "mod_added")
    bc_mm = Tick(nc, "mod_broadcast")
    h_done, hT_mm, hT_sb = Tick(nc, "h_done"), Tick(nc, "hT_in_psum"), Tick(nc, "hT_copied")
    const_done = Tick(nc, "constants_done")

    def mod_products(pe, first, cols, banks):
        for i in range(cols):
            w = arrived(pe, first + i)
            for k in range(KD):
                mm = nc.tensor.matmul(banks[i][0:DB + 1, :], cT[:, k, :], w[:, k, :], start=k == 0, stop=k == KD - 1)
            mod_mm.inc(mm)
            read_by(first + i, mod_mm)

    with nc.Block() as block:
        @block.gpsimd
        def _(pool):
            step = chained(pool, gch)

            def fill(out, value, *keeps):
                step(pool.memset(out, value[0]))
                for op, base, ch, pattern in keeps:
                    step(pool.affine_select(out=out, in_=out, compare_op=op, fill=value[1], base=base,
                                            pattern=pattern, channel_multiplier=ch))
            ge, eq = ALU.is_ge, ALU.is_equal
            fill(ident, (1.0, 0.0), (eq, 0, 1, [[-1, P]]))
            fill(selP, (1.0, 0.0), (ge, 0, -1, [[0, P]]))
            fill(selS.rearrange("p (b t) -> p b t", b=DB), (1.0, 0.0), (eq, -1, 1, [[-1, DB], [0, DS]]))
            const_done.inc(pool.memset(ones, 1.0))
            fill(cumU, (1.0, 0.0), (ge, 0, -1, [[1, P]]))
            fill(causneg, (0.0, NEG), (ge, 0, 1, [[-1, P]]))
            same = lambda n, b: [(ge, 0, 1, [[-b, n], [0, b]]), (ge, b - 1, -1, [[b, n], [0, b]])]
            c2 = lambda v: v.rearrange("p (n r) -> p n r", n=2)
            fill(c2(chunk1), (1.0, 0.0), *same(2, 64))
            fill(c2(chunkU), (1.0, 0.0), *same(2, 64))
            step(pool.affine_select(out=chunkU, in_=chunkU, compare_op=ge, fill=0.0, base=0, pattern=[[1, P]], channel_multiplier=-1))
            fill(c2(decneg), (0.0, NEG), *same(2, 64))
            step(pool.affine_select(out=decneg, in_=decneg, compare_op=ge, fill=NEG, base=0, pattern=[[1, P]], channel_multiplier=-1))
            fill(strictL, (1.0, 0.0), (ge, -1, 1, [[-1, P]]))
            fill(strictU, (1.0, 0.0), (ge, -1, -1, [[1, P]]))
            for l in range(6):
                b = 2 << l
                n = P // b
                fill(lvl[:, l, :].rearrange("p (n r) -> p n r", n=n), (1.0, 0.0), (ge, 0, 1, [[-b, n], [0, b]]),
                     (ge, b // 2 - 1, -1, [[b, n], [0, b]]), (ge, -(b // 2), 0, [[0, n], [1, b]]))
            fill(E8, (1.0, 0.0), (eq, 0, 1, [[-1, H], [0, P]]))
            fill(EH.rearrange("p (t h) -> p t h", h=H), (1.0, 0.0), (eq, 0, 1, [[0, DS], [-1, H]]))
            s4 = sampU.rearrange("p (n r) -> p n r", n=DB)
            fill(s4, (1.0, 0.0), *same(DB, DS))
            step(pool.affine_select(out=sampU, in_=sampU, compare_op=ge, fill=0.0, base=0, pattern=[[1, NS_TOK]], channel_multiplier=-1))
            fill(R, (1.0, 0.0), (ge, 0, 1, [[-H, DS]]), (ge, H - 1, -1, [[H, DS]]))
            fill(MB4, (1.0, 0.0), (eq, 0, 1, [[-1, H], [-H, DS]]))
            n4 = newneg.rearrange("p b (c m) -> p b c m", m=DS)
            fill(n4, (0.0, NEG), (eq, 0, 0, [[1, DB], [-1, DB], [0, DS]]), (ge, 0, 1, [[0, DB], [0, DB], [-H, DS]]))
            step(pool.memset(sm, 0.0))
            step(pool.memset(bias24[:, 0:8], 0.0))
            step(pool.memset(QB, 0.0))

        @block.scalar
        def _(act):
            cload.inc(act.dma_start(call[0:1, :], A["c_prompt"]), 16)
            cload.inc(act.dma_start(call[1:DB + 1, :], A["c_sample"]), 16)
            cload.inc(act.dma_start(modb, A["b_ada"][0:1, 0:2 * D].broadcast_to([DB + 1, 2 * D])), 16)
            xload.inc(act.dma_start(x_tm[:, 0:PT, :], A["x_prompt"][0].rearrange("(t p) d -> p t d", p=P)), 16)
            xload.inc(act.dma_start(x_tm[0:NS_TOK, PT, :], A["x_sample"].rearrange("b t d -> (b t) d")), 16)
            small.inc(act.dma_start(w24[:, :, 0:16], w_in[:, :, COL["b"]:COL["b"] + 16]), 16)
            small.inc(act.dma_start(w24[:, :, 16:24], w_in[:, :, COL["f"]:COL["f"] + 8]), 16)
            small.inc(act.dma_start(bias24[:, 8:16], A["gdn_dt_bias"].broadcast_to([P, H])), 16)
            small.inc(act.dma_start(bias24[:, 16:24], A["fox_f_bias"].broadcast_to([P, H])), 16)
            small.inc(act.dma_start(nega, A["gdn_a_log"].broadcast_to([P, H])), 16)
            small.inc(act.dma_start(normg, A["gdn_norm_g"].broadcast_to([P, HD])), 16)
            for t in range(NT):
                n = TOKS[t]
                for half in range(2):
                    act.wait_ge(hT_mm.sem, 2 * t + half + 1)
                    src = bank[4 + (2 * t + half) % 4][:, 0:4 * n].rearrange("p (k n) -> p k n", k=4)
                    hT_sb.inc(nc.scalar.copy(hT[:, 4 * half:4 * half + 4, t * P:t * P + n], src))

        @block.tensor
        def _(pe):
            pe.wait_ge(cload.sem, 48)
            pe.wait_ge(const_done.sem, 1)
            for k in range(KD):
                mm = nc.tensor.transpose(bank[4][:, k * 9:k * 9 + 9], call[:, k * P:(k + 1) * P], ident[0:DB + 1, 0:DB + 1])
            cT_ready.inc(mm)
            pe.wait_ge(cT_sb.sem, 1)
            mod_products(pe, 0, 4, bank[0:4])
            pe.wait_ge(mod_sb.sem, 4)
            for kind, sel, n in ((0, selP, P), (1, selS, NS_TOK)):
                if kind:
                    pe.wait_ge(h_done.sem, PT)
                for i in range(4):
                    mm = nc.tensor.matmul(bank[i][0:n, :], sel, modb[:, 512 * i:512 * i + 512], start=True, stop=True)
                bc_mm.inc(mm)
                for t in (range(PT) if not kind else (PT,)):
                    pe.wait_ge(h_done.sem, t + 1)
                    for half in range(2):
                        j = 2 * t + half
                        if j >= 4:
                            pe.wait_ge(hT_sb.sem, j - 3)
                        for k in range(4):
                            kk = 4 * half + k
                            mm = nc.tensor.transpose(bank[4 + j % 4][:, k * n:(k + 1) * n],
                                                     h_tm[t % 2][0:n, kk * P:(kk + 1) * P], ident[0:n, 0:n])
                        hT_mm.inc(mm)

        @block.sync
        def _(sp):
            send_until(sp, 7)

        @block.vector
        def _(dve):
            step = chained(dve, vch)
            dve.wait_ge(cT_ready.sem, 1)
            cT_sb.inc(nc.vector.tensor_copy(cT, bank[4][:, 0:72].rearrange("p (k n) -> p k n", k=KD)))
            for i in range(4):
                dve.wait_ge(mod_mm.sem, i + 1)
                m = modb[:, 512 * i:512 * i + 512]
                mod_sb.inc(nc.vector.tensor_tensor(m, bank[i][0:DB + 1, :], m, ALU.add))
            dve.wait_ge(xload.sem, 32)
            for t in range(NT):
                n = TOKS[t]
                dve.wait_ge(bc_mm.sem, 1 + t // PT)
                if t >= 2:
                    dve.wait_ge(hT_mm.sem, 2 * (t - 1))
                for i in range(2):
                    cols = slice(512 * i, 512 * i + 512)
                    step(nc.vector.scalar_tensor_tensor(h_tm[t % 2][0:n, cols], bank[2 + i][0:n, :], 1.0,
                                                        x_tm[0:n, t, cols], ALU.add, ALU.mult))
                    ins = nc.vector.tensor_tensor(h_tm[t % 2][0:n, cols], h_tm[t % 2][0:n, cols], bank[i][0:n, :], ALU.add)
                    step(ins) if i == 0 else h_done.inc(ins)
            dve.wait_ge(gch.sem, gch.n)
            step(nc.vector.tensor_reduce(MB, MB4, AX.X, ALU.add))

    fq, fk = at(T1, CW, TOK), at(T1 + 2176, CW, TOK)
    k_tm, v_tm = at(T1 + 4352, NT, W), at(T1 + 6912, NT, W)
    spt = at(T2 + 1024, 3, NT, 24)
    fq_mm, fq_sb = Tick(nc, "fox_q_product"), Tick(nc, "fox_q_copied")
    fk_mm, fk_sb = Tick(nc, "fox_k_product"), Tick(nc, "fox_k_copied")
    fv_mm, fv_sb = Tick(nc, "fox_v_product"), Tick(nc, "fox_v_copied")
    sm_mm, gate_y, gate_l = Tick(nc, "gates_product"), Tick(nc, "gates_y"), Tick(nc, "gates_log")
    lf_done = Tick(nc, "logf_done")
    ktm_mm, ktm_sb = Tick(nc, "k_rows_in_psum"), Tick(nc, "k_rows_copied")
    nF_mm, nF_sb = Tick(nc, "forget_sum"), Tick(nc, "forget_sum_copied")
    lf_load = Tick(nc, "past_logf_loaded")

    def feature_major(w, m, rhs, pair, kt=KD):
        for i in range(2):
            for k in range(kt):
                mm = nc.tensor.matmul(pair[i][:, 0:HALF], w[:, k, m * P:(m + 1) * P],
                                      rhs[:, k, i * HALF:(i + 1) * HALF], start=k == 0, stop=k == kt - 1)
        return mm

    def token_major(out, t, lhs, w, cols, kt=KD):
        n = TOKS[t]
        for k in range(kt):
            mm = nc.tensor.matmul(out, lhs[:, k, t * P:t * P + n], w[:, k, cols], start=k == 0, stop=k == kt - 1)
        return mm

    with nc.Block() as block:
        @block.tensor
        def _(pe):
            w = arrived(pe, 4)
            for m in range(CW):
                mm = feature_major(w, m, hT, bank[2 * m:2 * m + 2])
                fq_mm.inc(mm)
            read_by(4, fq_mm)
            w = arrived(pe, 5)
            for m in range(CW):
                pe.wait_ge(fq_sb.sem, m + 1)
                mm = feature_major(w, m, hT, bank[2 * m:2 * m + 2])
                fk_mm.inc(mm)
            read_by(5, fk_mm)
            w = arrived(pe, 6)
            for t in range(NT):
                pe.wait_ge(fk_sb.sem, t // 2 + 1)
                mm = token_major(bank[t][0:TOKS[t], :], t, hT, w, slice(0, W))
                fv_mm.inc(mm)
            read_by(6, fv_mm)
            pe.wait_ge(small.sem, 96)
            pe.wait_ge(fk_sb.sem, CW)
            for t in range(NT):
                mm = token_major(bank[7][0:TOKS[t], 24 * t:24 * t + 24], t, hT, w24, slice(0, 24))
            sm_mm.inc(mm)
            for t in range(NT):
                pe.wait_ge(fv_sb.sem, t + 1)
                n = TOKS[t]
                for cc in range(CW):
                    mm = nc.tensor.transpose(bank[t][0:n, cc * P:(cc + 1) * P], fk[:, cc, t * P:t * P + n], ident)
                ktm_mm.inc(mm)
            pe.wait_ge(lf_done.sem, 1)
            for t in range(PT):
                for s in range(t + 1):
                    nc.tensor.matmul(bank[5][0:H, t * P:(t + 1) * P], logf[:, s, :], cumU if s == t else ones,
                                     start=s == 0, stop=s == t)
            nF_mm.inc(nc.tensor.matmul(bank[6][0:H, 0:NS_TOK], logf[0:NS_TOK, PT, :], sampU, start=True, stop=True))

        @block.sync
        def _(sp):
            send_until(sp, 10)
            for b in range(DB):
                for g in range(NPG):
                    page = sp.value_load(A["page_table"][b:b + 1, g:g + 1], min_val=0, max_val=NPHYS - 1)
                    lf_load.inc(sp.dma_start(lfp[:, b * NPG + g, :].unsqueeze(1), A["cache_logf"][0, bass.ds(page, 1)].rearrange("a p h -> p a h")), 16)
            sp.wait_ge(ktm_sb.sem, NT)
            kp = A["k_prompt"][0, 0].rearrange("(t p) h d -> p t (h d)", p=P)
            stored.inc(sp.dma_start(kp, k_tm[:, 0:PT, :]), 16)
            stored.inc(sp.dma_start(A["k_sample"][0].rearrange("b t h d -> (b t) (h d)"), k_tm[0:NS_TOK, PT, :]), 16)
            sp.wait_ge(fv_sb.sem, NT)
            vp = A["v_prompt"][0, 0].rearrange("(t p) h d -> p t (h d)", p=P)
            stored.inc(sp.dma_start(vp, v_tm[:, 0:PT, :]), 16)
            stored.inc(sp.dma_start(A["v_sample"][0].rearrange("b t h d -> (b t) (h d)"), v_tm[0:NS_TOK, PT, :]), 16)
            sp.wait_ge(lf_done.sem, 1)
            stored.inc(sp.dma_start(A["logf_prompt"][0, 0].rearrange("(t p) h -> p t h", p=P), logf[:, 0:PT, :]), 16)
            stored.inc(sp.dma_start(A["logf_sample"][0].rearrange("b t h -> (b t) h"), logf[0:NS_TOK, PT, :]), 16)

        @block.scalar
        def _(act):
            step = chained(act, ach)
            for m in range(CW):
                act.wait_ge(fq_mm.sem, m + 1)
                step(nc.scalar.mul(fq[:, m, 0:HALF], bank[2 * m][:, 0:HALF], SCALE))
                fq_sb.inc(nc.scalar.mul(fq[:, m, HALF:TOK], bank[2 * m + 1][:, 0:HALF], SCALE))
            for t in range(NT):
                act.wait_ge(fv_mm.sem, t + 1)
                fv_sb.inc(nc.scalar.copy(v_tm[0:TOKS[t], t, :], bank[t][0:TOKS[t], :]))
            act.wait_ge(gate_y.sem, 1)
            step(nc.scalar.activation(spt[:, 0], sm, ACT.Abs))
            step(nc.scalar.activation(spt[:, 1], spt[:, 0], ACT.Exp, scale=-1.0))
            step(nc.scalar.activation(nega, nega, ACT.Exp))
            gate_l.inc(nc.scalar.activation(spt[:, 0, :, 0:H], sm[:, :, 0:H], ACT.Exp, scale=-1.0))
            act.wait_ge(gate_y.sem, 2)
            gate_l.inc(nc.scalar.activation(spt[:, 2], spt[:, 1], ACT.Ln))
            act.wait_ge(nF_mm.sem, 1)
            step(nc.scalar.mul(nF[:, 0:SEQ], bank[5][0:H, :], -1.0))
            nF_sb.inc(nc.scalar.mul(nF[:, SEQ:TOK], bank[6][0:H, 0:NS_TOK], -1.0))

        @block.vector
        def _(dve):
            step = chained(dve, vch)
            for m in range(CW):
                dve.wait_ge(fk_mm.sem, m + 1)
                step(nc.vector.tensor_copy(fk[:, m, 0:HALF], bank[2 * m][:, 0:HALF]))
                fk_sb.inc(nc.vector.tensor_copy(fk[:, m, HALF:TOK], bank[2 * m + 1][:, 0:HALF]))
            dve.wait_ge(sm_mm.sem, 1)
            dve.wait_ge(small.sem, 96)
            b24 = lambda n: bias24[0:n].unsqueeze(1)
            src = bank[7][:, 0:24 * PT].rearrange("p (t n) -> p t n", t=PT)
            step(nc.vector.tensor_tensor(sm[:, 0:PT, :], src, b24(P).to_broadcast([P, PT, 24]), ALU.add))
            gate_y.inc(nc.vector.tensor_tensor(sm[0:NS_TOK, PT, :], bank[7][0:NS_TOK, 24 * PT:24 * NT], bias24[0:NS_TOK], ALU.add))
            dve.wait_ge(gate_l.sem, 1)
            step(nc.vector.tensor_scalar(beta, spt[:, 0, :, 0:H], 1.0, None, ALU.add))
            step(nc.vector.reciprocal(beta, beta))
            gate_y.inc(nc.vector.tensor_scalar(spt[:, 1], spt[:, 1], 1.0, None, ALU.add))
            dve.wait_ge(gate_l.sem, 2)
            lf_done.inc(nc.vector.scalar_tensor_tensor(logf, sm[:, :, 16:24], 0.0, spt[:, 2, :, 16:24], ALU.min, ALU.subtract))
            step(nc.vector.scalar_tensor_tensor(gdec, sm[:, :, 8:16], 0.0, spt[:, 2, :, 8:16], ALU.max, ALU.add))
            step(nc.vector.scalar_tensor_tensor(gdec, gdec, -1.0, nega.unsqueeze(1).to_broadcast([P, NT, H]), ALU.mult, ALU.mult))
            for t in range(NT):
                dve.wait_ge(ktm_mm.sem, t + 1)
                n = TOKS[t]
                ktm_sb.inc(nc.vector.tensor_copy(k_tm[0:n, t, :], bank[t][0:n, :]))

    prob = [at(T1 + 9472 + 512 * i, PT, P) for i in range(2)]
    probT = [at(T1 + 10496 + 512 * i, PT, P) for i in range(2)]
    o_rows = at(T2 + 1400, W)
    KV = [at(T2 + 2000 + 2048 * i, 2 * NPG, W) for i in range(2)]
    s_mm, s_max, s_exp = Tick(nc, "scores_product"), Tick(nc, "scores_max"), Tick(nc, "probs_done")
    pT_mm, pT_sb, pv_mm = Tick(nc, "probsT_in_psum"), Tick(nc, "probsT_copied"), Tick(nc, "values_product")
    o_norm, oT_mm, oT_sb = Tick(nc, "o_normalised"), Tick(nc, "oT_in_psum"), Tick(nc, "oT_copied")
    kv_load = [Tick(nc, f"pages_loaded{i}") for i in range(2)]
    JOBS = [(t, h) for t in range(PT) for h in range(H)]

    def load_pages(sp, b):
        for g in range(NPG):
            page = sp.value_load(A["page_table"][b:b + 1, g:g + 1], min_val=0, max_val=NPHYS - 1)
            for i, name in enumerate(("cache_k", "cache_v")):
                kv_load[b % 2].inc(sp.dma_start(KV[b % 2][:, NPG * i + g, :].unsqueeze(1), A[name][0, bass.ds(page, 1)].rearrange(
                    "a p h d -> p a (h d)")), 16)

    with nc.Block() as block:
        @block.sync
        def _(sp):
            for b in range(2):
                load_pages(sp, b)

        @block.tensor
        def _(pe):
            def scores(j):
                t, h = JOBS[j]
                if j >= 3:
                    pe.wait_ge(s_exp.sem, j - 2)
                n, r = P * (t + 1), slice(HD * (h % 2), HD * (h % 2) + HD)
                out = bank[j % 3][:, 0:n]
                nc.tensor.matmul(out, fq[r, h // 2, t * P:(t + 1) * P], fk[r, h // 2, 0:n], start=True, stop=False)
                s_mm.inc(nc.tensor.matmul(out, E8[:, h, :], nF[:, 0:n], start=False, stop=True))

            def out_transposes(t):
                pe.wait_ge(o_norm.sem, t + 1)
                if t:
                    pe.wait_ge(oT_sb.sem, t)
                for cc in range(CW):
                    mm = nc.tensor.transpose(bank[7][:, cc * P:(cc + 1) * P], o_rows[:, cc * P:(cc + 1) * P], ident)
                oT_mm.inc(mm)

            scores(0)
            for j, (t, h) in enumerate(JOBS):
                if j + 1 < len(JOBS):
                    scores(j + 1)
                pe.wait_ge(s_exp.sem, j + 1)
                if j >= 2:
                    pe.wait_ge(pT_sb.sem, j - 1)
                for s in range(t + 1):
                    mm = nc.tensor.transpose(bank[3 + j % 2][:, s * P:(s + 1) * P], prob[j % 2][:, s, :], ident)
                pT_mm.inc(mm)
                pe.wait_ge(pT_sb.sem, j + 1)
                if t >= 2 and h == 0:
                    pe.wait_ge(o_norm.sem, t - 1)
                for s in range(t + 1):
                    mm = nc.tensor.matmul(bank[5 + t % 2][:, h * HD:(h + 1) * HD], probT[j % 2][:, s, :],
                                          v_tm[:, s, h * HD:(h + 1) * HD], start=s == 0, stop=s == t)
                pv_mm.inc(mm)
                if t and h == 3:
                    out_transposes(t - 1)
            out_transposes(PT - 1)

        @block.vector
        def _(dve):
            step = chained(dve, vch)

            def normalise(t):
                dve.wait_ge(pv_mm.sem, H * (t + 1))
                if t:
                    dve.wait_ge(oT_mm.sem, t)
                cols = slice(H * t, H * t + H)
                step(nc.vector.reciprocal(rinv[:, cols], rsum[:, cols]))
                src = bank[5 + t % 2].ap().rearrange("p (h d) -> p h d", h=H)
                o_norm.inc(nc.vector.tensor_tensor(o_rows.rearrange("p (h d) -> p h d", h=H), src,
                                                   rinv[:, cols].unsqueeze(2).to_broadcast([P, H, HD]), ALU.mult))
            for j, (t, h) in enumerate(JOBS):
                dve.wait_ge(s_mm.sem, j + 1)
                diag = bank[j % 3][:, t * P:(t + 1) * P]
                step(nc.vector.tensor_tensor(diag, diag, causneg, ALU.add))
                s_max.inc(nc.vector.tensor_reduce(nm[:, j:j + 1], bank[j % 3][:, 0:P * (t + 1)], AX.X, ALU.max, negate=True))
                if t and h == 1:
                    normalise(t - 1)
            normalise(PT - 1)

        @block.scalar
        def _(act):
            def take_oT(t):
                act.wait_ge(oT_mm.sem, t + 1)
                oT_sb.inc(nc.scalar.copy(oTb[:, :, t * P:(t + 1) * P], bank[7].ap().rearrange("p (c n) -> p c n", c=CW)))

            for j, (t, h) in enumerate(JOBS):
                act.wait_ge(s_max.sem, j + 1)
                if j >= 2:
                    act.wait_ge(pT_mm.sem, j - 1)
                n = P * (t + 1)
                s_exp.inc(nc.scalar.activation(prob[j % 2][:, 0:t + 1, :].rearrange("p s n -> p (s n)"), bank[j % 3][:, 0:n], ACT.Exp,
                                               bias=nm[:, j:j + 1], accum_out=rsum[:, j:j + 1]))
                act.wait_ge(pT_mm.sem, j + 1)
                if j >= 2:
                    act.wait_ge(pv_mm.sem, j - 1)
                pT_sb.inc(nc.scalar.copy(probT[j % 2][:, 0:t + 1, :].rearrange("p s n -> p (s n)"), bank[3 + j % 2][:, 0:n]))
                if t and h == 4:
                    take_oT(t - 1)
            take_oT(PT - 1)

        @block.gpsimd
        def _(pool):
            step = chained(pool, gch)
            for cc in range(CW):
                for par in range(2):
                    r = slice(HD * par, HD * par + HD)
                    dst = QB[r].rearrange("p (b c t) h -> p b c t h", b=DB, c=CW)[:, :, cc, :, 2 * cc + par]
                    step(nc.gpsimd.tensor_copy(dst, fq[r, cc, SEQ:TOK].rearrange("p (b t) -> p b t", b=DB)))

    NK = NPG * P + NS_TOK
    kT = [at(T1 + 9472 + 1024 * i, CW, NPG * P) for i in range(2)]
    z0 = T2 + 2000 + 4096
    suf = [at(z0 + 256 * i, NPG * P, p=H) for i in range(2)]
    ps_ = [at(z0 + 512 + NK * i, NK, p=NS_TOK) for i in range(2)]
    pTs = at(z0 + 512 + 2 * NK, 3, NS_TOK)
    om = at(z0 + 1200, W, p=NS_TOK)
    assert z0 + 1712 <= END, (z0 + 1712, END)
    kT_mm, kT_sb = Tick(nc, "past_keysT_in_psum"), Tick(nc, "past_keysT_copied")
    suf_mm, suf_sb = Tick(nc, "suffix_sum"), Tick(nc, "suffix_copied")
    ss_mm, ss_max, ss_exp, ss_n = (Tick(nc, n) for n in ("s_scores", "s_scores_max", "s_probs", "s_probs_normalised"))
    sp_mm, sp_sb, so_mm, so_sb, st_mm, st_sb = (Tick(nc, n) for n in (
        "s_probsT_in_psum", "s_probsT_copied", "s_values_product", "s_values_masked", "s_oT_in_psum", "s_oT_copied"))
    with nc.Block() as block:
        @block.sync
        def _(sp):
            for b in range(2, DB):
                sp.wait_ge(so_mm.sem, b - 1)
                load_pages(sp, b)
            sp.wait_ge(stored.sem, stored.n)

        @block.tensor
        def _(pe):
            def score(b):
                pe.wait_ge(kv_load[b % 2].sem, 16 * 4 * (b // 2 + 1))
                if b:
                    pe.wait_ge(kT_sb.sem, b)
                for cc in range(CW):
                    for g in range(NPG):
                        at_ = 256 * (cc % 2) + P * g
                        mm = nc.tensor.transpose(bank[cc // 2][:, at_:at_ + P], KV[b % 2][:, g, cc * P:(cc + 1) * P], ident)
                kT_mm.inc(mm)
                pe.wait_ge(lf_load.sem, 16 * DB * NPG)
                if b:
                    pe.wait_ge(suf_sb.sem, b)
                l0, l1 = lfp[:, NPG * b, :], lfp[:, NPG * b + 1, :]
                nc.tensor.matmul(bank[2][0:H, 0:P], l0, strictL, start=True, stop=False)
                nc.tensor.matmul(bank[2][0:H, 0:P], l1, ones, start=False, stop=True)
                suf_mm.inc(nc.tensor.matmul(bank[2][0:H, P:2 * P], l1, strictL, start=True, stop=True))
                pe.wait_ge(kT_sb.sem, b + 1)
                pe.wait_ge(suf_sb.sem, b + 1)
                if b >= 2:
                    pe.wait_ge(ss_exp.sem, b - 1)
                past, new = bank[3 + b % 2][0:NS_TOK, 0:NPG * P], bank[3 + b % 2][0:NS_TOK, NPG * P:NK]
                q = lambda cc: QB[:, (b * CW + cc) * DS:(b * CW + cc + 1) * DS, :].rearrange("p t h -> p (t h)")
                for cc in range(CW):
                    nc.tensor.matmul(past, q(cc), kT[b % 2][:, cc, :], start=cc == 0, stop=False)
                nc.tensor.matmul(past, EH, suf[b % 2], start=False, stop=True)
                for cc in range(CW):
                    nc.tensor.matmul(new, q(cc), fk[:, cc, SEQ:TOK], start=cc == 0, stop=False)
                ss_mm.inc(nc.tensor.matmul(new, EH, nF[:, SEQ:TOK], start=False, stop=True))

            def value(b):
                pe.wait_ge(ss_n.sem, b + 1)
                if b:
                    pe.wait_ge(sp_sb.sem, b)
                for g in range(NPG):
                    nc.tensor.transpose(bank[5][:, NS_TOK * g:NS_TOK * (g + 1)], ps_[b % 2][:, P * g:P * (g + 1)], ident[0:NS_TOK, 0:NS_TOK])
                sp_mm.inc(nc.tensor.transpose(bank[5][0:NS_TOK, 64:96], ps_[b % 2][:, 256:288], ident[0:NS_TOK, 0:NS_TOK]))
                pe.wait_ge(sp_sb.sem, b + 1)
                if b:
                    pe.wait_ge(so_sb.sem, b)
                for g in range(NPG):
                    mm = nc.tensor.matmul(bank[6][0:NS_TOK, :], pTs[:, g, :], KV[b % 2][:, NPG + g, :], start=g == 0, stop=False)
                mm = nc.tensor.matmul(bank[6][0:NS_TOK, :], pTs[0:NS_TOK, 2, :], v_tm[0:NS_TOK, PT, :], start=False, stop=True)
                so_mm.inc(mm)
                pe.wait_ge(so_sb.sem, b + 1)
                for cc in range(CW):
                    a = NS_TOK * cc + DS * b
                    mm = nc.tensor.matmul(bank[7][:, a:a + DS], om[:, cc * P:(cc + 1) * P], R, start=True, stop=True)
                st_mm.inc(mm)
            for b in range(DB + 1):
                if b < DB:
                    score(b)
                if b:
                    value(b - 1)

        @block.scalar
        def _(act):
            def take(b):
                act.wait_ge(kT_mm.sem, b + 1)
                if b >= 2:
                    act.wait_ge(ss_mm.sem, b - 1)
                for i in range(2):
                    ins = nc.scalar.copy(kT[b % 2][:, 2 * i:2 * i + 2, :], bank[i].ap().rearrange("p (c n) -> p c n", c=2))
                    kT_sb.inc(ins) if i else ach.inc(ins)
            for b in range(DB):
                take(b)
                act.wait_ge(ss_max.sem, b + 1)
                if b >= 2:
                    act.wait_ge(sp_mm.sem, b - 1)
                ss_exp.inc(nc.scalar.activation(ps_[b % 2], bank[3 + b % 2][0:NS_TOK, 0:NK], ACT.Exp,
                                                bias=nm[0:NS_TOK, b:b + 1], accum_out=rsum[0:NS_TOK, b:b + 1]))
            act.wait_ge(st_mm.sem, DB)
            st_sb.inc(nc.scalar.copy(oTb[:, :, SEQ:TOK], bank[7][:, 0:CW * NS_TOK].rearrange("p (c n) -> p c n", c=CW)))

        @block.vector
        def _(dve):
            step = chained(dve, vch)
            def front(b):
                dve.wait_ge(suf_mm.sem, b + 1)
                if b >= 2:
                    dve.wait_ge(ss_mm.sem, b - 1)
                suf_sb.inc(nc.vector.tensor_copy(suf[b % 2], bank[2][0:H, 0:256]))
                dve.wait_ge(ss_mm.sem, b + 1)
                new = bank[3 + b % 2][0:NS_TOK, NPG * P:NK]
                step(nc.vector.tensor_tensor(new, new, newneg[:, b, :], ALU.add))
                ss_max.inc(nc.vector.tensor_reduce(nm[0:NS_TOK, b:b + 1], bank[3 + b % 2][0:NS_TOK, 0:NK], AX.X, ALU.max, negate=True))
                dve.wait_ge(ss_exp.sem, b + 1)
                step(nc.vector.reciprocal(rinv[0:NS_TOK, b:b + 1], rsum[0:NS_TOK, b:b + 1]))
                ss_n.inc(nc.vector.tensor_scalar(ps_[b % 2], ps_[b % 2], rinv[0:NS_TOK, b:b + 1], None, ALU.mult))

            def back(b):
                dve.wait_ge(sp_mm.sem, b + 1)
                if b:
                    dve.wait_ge(so_mm.sem, b)
                step(nc.vector.tensor_copy(pTs[:, 0:2, :], bank[5][:, 0:64].rearrange("p (g n) -> p g n", g=2)))
                sp_sb.inc(nc.vector.tensor_copy(pTs[0:NS_TOK, 2, :], bank[5][0:NS_TOK, 64:96]))
                dve.wait_ge(so_mm.sem, b + 1)
                if b:
                    dve.wait_ge(st_mm.sem, b)
                so_sb.inc(nc.vector.tensor_tensor(om.rearrange("p (h d) -> p h d", h=H), bank[6][0:NS_TOK, :].rearrange(
                    "p (h d) -> p h d", h=H), MB.unsqueeze(2).to_broadcast([NS_TOK, H, HD]), ALU.mult))
            for b in range(DB + 1):
                if b < DB:
                    front(b)
                if b:
                    back(b - 1)

    SAMP = DB * (CONV - 1 + DS)
    PRE = CONV - 1 + SEQ
    NH = DB * (CONV - 1)
    qkv_tm, z_tm = at(T1, NT, 3 * W), at(T1 + 7680, NT, W)
    pre = [at(T1 + 10240 + 572 * i, PRE + SAMP) for i in range(2)]
    post = [at(T1 + 11384, TOK), at(T2, TOK)]
    hist, histT = at(T2 + 600, 3 * W, p=NH + CONV), at(T2 + 2136, CT, NH + CONV)
    cnew, cnew_rows = at(T2 + 2500, CT, CONV - 1 + NH), at(T2 + 2900, 3 * W, p=CONV - 1 + NH)
    hist_load, hist_mm, hist_sb = Tick(nc, "history_loaded"), Tick(nc, "historyT_in_psum"), Tick(nc, "historyT_copied")
    cp_mm, cp_sb, conv_sum, conv_act = (Tick(nc, n) for n in ("conv_in_product", "conv_in_copied", "conv_summed", "conv_silu"))
    row_mm, row_sb, z_mm, z_sb, row_zero = (Tick(nc, n) for n in (
        "qkv_rows_in_psum", "qkv_rows_copied", "z_product", "z_silu", "qkv_rows_zeroed"))
    cn_mm, cn_sb = Tick(nc, "conv_state_in_psum"), Tick(nc, "conv_state_copied")

    def windows(buf):
        return buf[:, 0:PRE], buf[:, PRE:PRE + SAMP].rearrange("p (b n) -> p b n", b=DB)

    with nc.Block() as block:
        @block.tensor
        def _(pe):
            pe.wait_ge(hist_load.sem, 32)
            n = NH + CONV
            for m in range(CT):
                mm = nc.tensor.transpose(bank[7][:, m * n:(m + 1) * n], hist[:, m * P:(m + 1) * P], ident[0:n, 0:n])
            hist_mm.inc(mm)

            def rows(m):
                pe.wait_ge(conv_act.sem, m + 1)
                if m:
                    pe.wait_ge(row_sb.sem, m)
                if m == 0:
                    pe.wait_ge(hist_sb.sem, 1)
                for t in range(NT):
                    n = TOKS[t]
                    out = bank[6][:, t * P:(t + 1) * P] if t < PT else bank[7][0:n, 0:P]
                    mm = nc.tensor.transpose(out, post[m % 2][:, t * P:t * P + n], ident)
                row_mm.inc(mm)

            for m in range(CT):
                w = arrived(pe, 7 + m // 4)
                if m >= 3:
                    pe.wait_ge(cp_sb.sem, m - 2)
                a = 2 * (m % 3)
                cp_mm.inc(feature_major(w, m % 4, hT, bank[a:a + 2]))
                if m % 4 == 3:
                    read_by(7 + m // 4, cp_mm)
                if m >= 2:
                    rows(m - 2)
            w = arrived(pe, 10)
            for t in range(NT):
                pe.wait_ge(cp_sb.sem, CT)
                z_mm.inc(token_major(bank[t][0:TOKS[t], :], t, hT, w, slice(0, W)))
                if t < 2:
                    rows(CT - 2 + t)
            read_by(10, z_mm)
            pe.wait_ge(row_sb.sem, CT)
            pe.wait_ge(z_sb.sem, 3)
            n = CONV - 1 + NH
            for m in range(CT):
                mm = nc.tensor.transpose(bank[m // 4][0:n, (m % 4) * P:(m % 4 + 1) * P], cnew[:, m, :], ident)
            cn_mm.inc(mm)

        @block.sync
        def _(sp):
            hist_load.inc(sp.dma_start(hist[0:NH, :], A["state_conv"][0].rearrange("b i c -> (b i) c")), 16)
            hist_load.inc(sp.dma_start(hist[NH:NH + CONV, :], A["conv_w"][0]), 16)
            send_until(sp, GATES)
            sp.wait_ge(cn_sb.sem, 1)
            n = CONV - 1
            stored.inc(sp.dma_start(A["conv_prompt"][0, 0], cnew_rows[0:n, :]), 16)
            stored.inc(sp.dma_start(A["conv_sample"][0].rearrange("b i c -> (b i) c"), cnew_rows[n:n + NH, :]), 16)

        @block.gpsimd
        def _(pool):
            row_zero.inc(pool.memset(qkv_tm[:, PT, :], 0.0))
            row_zero.inc(pool.memset(z_tm[:, PT, :], 0.0))
            for i in range(2):
                row_zero.inc(pool.memset(pre[i][:, 0:CONV - 1], 0.0))

        @block.scalar
        def _(act):
            step = chained(act, ach)
            act.wait_ge(hist_mm.sem, 1)
            hist_sb.inc(nc.scalar.copy(histT, bank[7][:, 0:CT * (NH + CONV)].rearrange("p (m n) -> p m n", m=CT)))
            act.wait_ge(hist_sb.sem, 1)

            def silu(m):
                act.wait_ge(conv_sum.sem, m + 1)
                conv_act.inc(nc.scalar.activation(post[m % 2], post[m % 2], ACT.Silu))
            for m in range(CT):
                act.wait_ge(cp_mm.sem, m + 1)
                if m >= 2:
                    act.wait_ge(conv_sum.sem, m - 1)
                a = 2 * (m % 3)
                run, seqs = windows(pre[m % 2])
                act.wait_ge(row_zero.sem, 4)
                step(nc.scalar.copy(run[:, CONV - 1:CONV - 1 + HALF], bank[a][:, 0:HALF]))
                step(nc.scalar.copy(run[:, CONV - 1 + HALF:PRE], bank[a + 1][:, 0:SEQ - HALF]))
                step(nc.scalar.copy(seqs[:, :, 0:CONV - 1], histT[:, m, 0:NH].rearrange("p (b i) -> p b i", b=DB)))
                cp_sb.inc(nc.scalar.copy(seqs[:, :, CONV - 1:], bank[a + 1][:, SEQ - HALF:HALF].rearrange("p (b t) -> p b t", b=DB)))
                if m:
                    silu(m - 1)
            silu(CT - 1)
            for t in range(NT):
                act.wait_ge(z_mm.sem, t + 1)
                z_sb.inc(nc.scalar.activation(z_tm[0:TOKS[t], t, :], bank[t][0:TOKS[t], :], ACT.Silu))

        @block.vector
        def _(dve):
            step = chained(dve, vch)
            dve.wait_ge(hist_sb.sem, 1)
            dve.wait_ge(row_zero.sem, 4)

            def take_rows(m):
                dve.wait_ge(row_mm.sem, m + 1)
                cols = slice(m * P, (m + 1) * P)
                step(nc.vector.tensor_copy(qkv_tm[:, 0:PT, cols], bank[6].ap().rearrange("p (t n) -> p t n", t=PT)))
                done(row_sb, nc.vector.tensor_copy(qkv_tm[0:NS_TOK, PT, cols], bank[7][0:NS_TOK, 0:P]))
            for m in range(CT):
                dve.wait_ge(cp_sb.sem, m + 1)
                if m >= 2:
                    dve.wait_ge(row_mm.sem, m - 1)
                run, seqs = windows(pre[m % 2])
                out = post[m % 2]
                outs = out[:, SEQ:TOK].rearrange("p (b t) -> p b t", b=DB)
                step(nc.vector.tensor_copy(cnew[:, m, 0:CONV - 1], run[:, SEQ:PRE]))
                step(nc.vector.tensor_copy(cnew[:, m, CONV - 1:].rearrange("p (b i) -> p b i", b=DB), seqs[:, :, DS:]))
                for i in range(CONV):
                    wi = histT[:, m, NH + i:NH + i + 1]
                    if i == 0:
                        step(nc.vector.tensor_scalar(out[:, 0:SEQ], run[:, 0:SEQ], wi, None, ALU.mult))
                        step(nc.vector.tensor_scalar(outs, seqs[:, :, 0:DS], wi, None, ALU.mult))
                    else:
                        step(nc.vector.scalar_tensor_tensor(out[:, 0:SEQ], run[:, i:i + SEQ], wi, out[:, 0:SEQ], ALU.mult, ALU.add))
                        ins = nc.vector.scalar_tensor_tensor(outs, seqs[:, :, i:i + DS], wi, outs, ALU.mult, ALU.add)
                        done(conv_sum, ins) if i == CONV - 1 else step(ins)
                if m >= 2:
                    take_rows(m - 2)
            for m in (CT - 2, CT - 1):
                take_rows(m)
            dve.wait_ge(cn_mm.sem, 1)
            n = CONV - 1 + NH
            for i in range(3):
                ins = nc.vector.tensor_copy(cnew_rows[:, 512 * i:512 * i + 512], bank[i][0:n, :])
                cn_sb.inc(ins) if i == 2 else step(ins)

    tmp1 = at(T2 + 512, 2 * W)
    ss = at(T2 + 1600, NT, 2 * H)
    gs = at(T2 + 7424, 4, PT, H)
    G, gam, kdf = (gs[:, i] for i in range(3))
    glast = gs[:, 3].rearrange("p t h -> p (t h)").rearrange("p (c t h) -> p c t h", c=2, t=PT)
    GT = nF[:, 0:SEQ]
    ab = at(T2 + 7560, H, 2, p=NS_TOK)
    sq_sum, sq_root = Tick(nc, "squares_summed"), Tick(nc, "norms_rooted")
    g_mm, g_sb, g_exp = Tick(nc, "decay_sums"), Tick(nc, "decay_sums_copied"), Tick(nc, "decays_done")
    normed, ab_done = Tick(nc, "qk_normalised"), Tick(nc, "sample_gates_done")
    scr = nc.dram_tensor("sample_rows", (DB, H, DS, 3, HD), F32).ap()
    scr_ab = nc.dram_tensor("sample_gates", (DB, H, DS, 2), F32).ap()
    scr_o = nc.dram_tensor("sample_out", (DB, H, DS, HD), F32).ap()
    rows_out = Tick(nc, "sample_rows_stored")
    with nc.Block() as block:
        @block.tensor
        def _(pe):
            g4 = gdec[:, 0:PT, :]
            nc.tensor.matmul(bank[0][:, 0:32], chunkU, g4, start=True, stop=True)
            nc.tensor.matmul(bank[0][:, 32:64], chunk1, g4, start=True, stop=True)
            for cc in range(2):
                for par in range(2):
                    nc.tensor.matmul(bank[2][64 * par:64 * par + 64, 16 * cc:16 * cc + 16], chunk1[:, 64 * cc:64 * cc + 64],
                                     gdec[:, 0:PT, par::2], start=True, stop=True)
            for t in range(PT):
                mm = nc.tensor.matmul(bank[1][0:H, t * P:(t + 1) * P], gdec[:, t, :], chunkU, start=True, stop=True)
            g_mm.inc(mm)

        @block.vector
        def _(dve):
            step = chained(dve, vch)
            for t in range(NT):
                x = qkv_tm[:, t, 0:2 * W]
                step(nc.vector.tensor_tensor(tmp1, x, x, ALU.mult))
                step(nc.vector.tensor_reduce(ss[:, t, :], tmp1.rearrange("p (h d) -> p h d", d=HD), AX.X, ALU.add))
            done(sq_sum, nc.vector.tensor_scalar(ss, ss, RMS_EPS, None, ALU.add))
            dve.wait_ge(g_mm.sem, 1)
            step(nc.vector.tensor_copy(G, bank[0][:, 0:32].rearrange("p (t h) -> p t h", t=PT)))
            step(nc.vector.tensor_copy(gs[:, 3], bank[2][:, 0:32].rearrange("p (t h) -> p t h", t=PT)))
            step(nc.vector.tensor_copy(GT, bank[1][0:H, :]))
            done(g_sb, nc.vector.tensor_tensor(kdf, bank[0][:, 32:64].rearrange("p (t h) -> p t h", t=PT), G, ALU.subtract))
            dve.wait_ge(sq_root.sem, 1)
            step(nc.vector.reciprocal(ss, ss))
            step(nc.vector.tensor_scalar(ss[:, :, 0:H], ss[:, :, 0:H], HD ** -0.5, None, ALU.mult))
            for t in reversed(range(NT)):
                x = qkv_tm[:, t, 0:2 * W].rearrange("p (h d) -> p h d", d=HD)
                done(normed, nc.vector.tensor_tensor(x, x, ss[:, t, :].unsqueeze(2).to_broadcast([P, 2 * H, HD]), ALU.mult))

        @block.scalar
        def _(act):
            step = chained(act, ach)
            step(nc.scalar.copy(ab[:, :, 0], beta[0:NS_TOK, PT, :]))
            ab_done.inc(nc.scalar.activation(ab[:, :, 1], gdec[0:NS_TOK, PT, :], ACT.Exp))
            act.wait_ge(g_sb.sem, 1)
            step(nc.scalar.activation(gam, G, ACT.Exp))
            g_exp.inc(nc.scalar.activation(gs[:, 2:4], gs[:, 2:4], ACT.Exp))
            act.wait_ge(sq_sum.sem, 1)
            sq_root.inc(nc.scalar.activation(ss, ss, ACT.Sqrt))

        @block.sync
        def _(sp):
            sp.wait_ge(ab_done.sem, 1)
            for b in range(DB):
                rows_out.inc(sp.dma_start(scr_ab[b].rearrange("h t c -> t h c"), ab[DS * b:DS * b + DS]), 16)
            sp.wait_ge(normed.sem, 1)
            for b in range(DB):
                for i in range(3):
                    rows_out.inc(sp.dma_start(scr[b, :, :, i].rearrange("h t d -> t h d"),
                                              qkv_tm[DS * b:DS * b + DS, PT, W * i:W * i + W].rearrange("p (h d) -> p h d", h=H)), 16)
            sp.wait_ge(stored.sem, stored.n)

    trT = at(X0 + 9472, 4, CW, P)
    rows4 = at(T1 + 10240, 4, W)
    kd = at(T2, W)
    LT, dec, Lm, Tm, Um, P1 = (at(T2 + 512 + 1024 * i, H, P) for i in range(6))
    w1, nw2T = rows4[:, 0], rows4[:, 1].rearrange("p (c n) -> p c n", c=CW)
    S = at(T2 + 6656, CW, HD)
    u = at(T2 + 6912, W)
    sS, stmp = at(0, HD, 32), at(2048, HD, 32)
    sx = at(X0 + 13696, DS, 3, HD)
    sab, snab = at(X0 + 13696 + 768, DS, 2), at(X0 + 13696 + 776, DS)
    sv, so, skv = at(X0 + 13696 + 784, DS, 32), at(X0 + 13696 + 912, DS, 32), at(X0 + 13696 + 1040, 32)
    in_load, s_zero = Tick(nc, "sample_state_loaded"), Tick(nc, "state_zeroed")
    r_done, tr_mm, tr_sb, kk_mm, gr_mm, dec_sub, dec_exp, lt_done = (Tick(nc, n) for n in (
        "scaled_rows", "gdn_T_in_psum", "gdn_T_copied", "kk_product", "decay_rows", "decay_diffs", "decay_matrix", "LT_done"))
    lm_done, p1_mm, p1_sb, q_mm, u_sb, t_mm, t_sb = (Tick(nc, n) for n in (
        "level_masked", "LT_product", "LT_product_copied", "TLT_product", "inverse_updated", "inverse_T", "inverse_T_copied"))
    w_mm, w1_sb, w2_sb, un_mm, un_sb, od_mm, st_sb2, o_sb = (Tick(nc, n) for n in (
        "w_products", "w1_copied", "w2_copied", "state_read", "u_done", "o_product", "state_updated", "o_copied"))
    srec, so_back = Tick(nc, "sample_recurrence"), Tick(nc, "sample_out_moved")
    NL = 6
    with nc.Block() as block:
        @block.tensor
        def _(pe):
            for t in range(PT):
                pe.wait_ge(r_done.sem, 3 * t + 2)
                if t:
                    pe.wait_ge(o_sb.sem, t)
                srcs = [qkv_tm[:, t, W:2 * W], rows4[:, 0], qkv_tm[:, t, 0:W], rows4[:, 1]]
                for i, s in enumerate(srcs):
                    for cc in range(CW):
                        mm = nc.tensor.transpose(bank[i][:, cc * P:(cc + 1) * P], s[:, cc * P:(cc + 1) * P], ident)
                tr_mm.inc(mm)
                pe.wait_ge(tr_sb.sem, t + 1)
                for h in range(H):
                    nc.tensor.matmul(bank[h // 4][:, (h % 4) * P:(h % 4 + 1) * P], E8[:, h, :], GT[:, t * P:(t + 1) * P], start=True, stop=True)
                for h in range(H):
                    r = slice(HD * (h % 2), HD * (h % 2) + HD)
                    mm = nc.tensor.matmul(bank[4 + 2 * (h % 2) + h // 4][:, 256 * (h // 2 % 2):256 * (h // 2 % 2) + 256], trT[r, 0, h // 2, :],
                                          trT[r, 1:3, h // 2, :], start=True, stop=True)
                kk_mm.inc(mm)
                for l in range(NL):
                    for hb in range(2):
                        n = 2 * (NL * t + l) + hb
                        heads = range(4 * hb, 4 * hb + 4)
                        pe.wait_ge(lm_done.sem, n + 1)
                        col = lambda h: slice((h % 4) * P, (h % 4 + 1) * P)
                        if l == 0:
                            for h in heads:
                                mm = nc.tensor.transpose(bank[hb][:, col(h)], Lm[:, h, :], ident)
                            p1_mm.inc(mm)
                        else:
                            pe.wait_ge(t_sb.sem, 2 * ((NL - 1) * t + l - 1) + hb + 1)
                            for h in heads:
                                mm = nc.tensor.matmul(bank[hb][:, col(h)], Lm[:, h, :], Tm[:, h, :], start=True, stop=True)
                            p1_mm.inc(mm)
                    if l == 0:
                        continue
                    for hb in range(2):
                        heads = range(4 * hb, 4 * hb + 4)
                        k = 2 * ((NL - 1) * t + l - 1) + hb
                        pe.wait_ge(p1_sb.sem, k + 1)
                        for h in heads:
                            mm = nc.tensor.matmul(bank[2 + hb][:, col(h)], P1[:, h, :], Um[:, h, :], start=True, stop=True)
                        q_mm.inc(mm)
                    if l < NL - 1:
                        for hb in range(2):
                            heads = range(4 * hb, 4 * hb + 4)
                            pe.wait_ge(u_sb.sem, 2 * (NL * t + l) + hb + 1)
                            for h in heads:
                                mm = nc.tensor.transpose(bank[4 + hb][:, col(h)], Um[:, h, :], ident)
                            t_mm.inc(mm)
                pe.wait_ge(u_sb.sem, 2 * NL * (t + 1))
                pe.wait_ge(r_done.sem, 3 * t + 3)
                for h in range(H):
                    c64, r = slice(HD * h, HD * h + HD), slice(HD * (h % 2), HD * (h % 2) + HD)
                    nc.tensor.matmul(bank[6][:, c64], Um[:, h, :], rows4[:, 3, c64], start=True, stop=True)
                    mm = nc.tensor.matmul(bank[7][r, (h // 2) * P:(h // 2 + 1) * P], rows4[:, 2, c64], Um[:, h, :], start=True, stop=True)
                w_mm.inc(mm)
                pe.wait_ge(w1_sb.sem, t + 1)
                pe.wait_ge(w2_sb.sem, t + 1)
                half_of = lambda h: slice(HD * (h // 2), HD * (h // 2) + HD)
                for ch in range(2):
                    n = 2 * t + ch
                    pe.wait_ge(st_sb2.sem, n) if n else pe.wait_ge(s_zero.sem, 1)
                    k = slice(64 * ch, 64 * ch + 64)
                    for h in range(H):
                        c64, r = slice(HD * h, HD * h + HD), slice(HD * (h % 2), HD * (h % 2) + HD)
                        mm = nc.tensor.matmul(bank[3 * (h % 2)][k, half_of(h)], nw2T[r, h // 2, k], S[r, h // 2, :], start=True, stop=True)
                    un_mm.inc(mm)
                    pe.wait_ge(un_sb.sem, 2 * n + 2)
                    for h in range(H):
                        c64, r = slice(HD * h, HD * h + HD), slice(HD * (h % 2), HD * (h % 2) + HD)
                        nc.tensor.matmul(bank[1 + 3 * (h % 2)][k, half_of(h)], trT[r, 3, h // 2, k], S[r, h // 2, :], start=True, stop=True)
                        nc.tensor.matmul(bank[5][k, c64], dec[k, h, k], u[k, c64], start=True, stop=True)
                        mm = nc.tensor.matmul(bank[2][r, (h // 2) * HD:(h // 2 + 1) * HD], kd[k, c64], u[k, c64], start=True, stop=True)
                    od_mm.inc(mm)

        @block.vector
        def _(dve):
            step = chained(dve, vch)
            hd = lambda v: v.rearrange("p (h d) -> p h d", h=H)
            wide = lambda v: v.unsqueeze(2).to_broadcast([P, H, HD])
            done(s_zero, nc.vector.memset(S, 0.0))
            for t in range(PT):
                q, k, v = (hd(qkv_tm[:, t, W * i:W * i + W]) for i in range(3))
                if t:
                    dve.wait_ge(od_mm.sem, 2 * t)
                done(r_done, nc.vector.tensor_tensor(hd(rows4[:, 0]), k, wide(beta[:, t, :]), ALU.mult))
                done(r_done, nc.vector.tensor_tensor(hd(rows4[:, 1]), q, wide(gam[:, t, :]), ALU.mult))
                step(nc.vector.tensor_tensor(hd(rows4[:, 3]), v, wide(beta[:, t, :]), ALU.mult))
                step(nc.vector.tensor_tensor(hd(kd), k, wide(kdf[:, t, :]), ALU.mult))
                done(r_done, nc.vector.tensor_tensor(hd(rows4[:, 2]), hd(rows4[:, 0]), wide(gam[:, t, :]), ALU.mult))
                dve.wait_ge(kk_mm.sem, t + 1)
                for i in range(2):
                    d4 = dec[:, 4 * i:4 * i + 4, :]
                    step(nc.vector.tensor_tensor(d4, bank[i].ap().rearrange("p (h n) -> p h n", h=4),
                                                 G[:, t, 4 * i:4 * i + 4].unsqueeze(2).to_broadcast([P, 4, P]), ALU.subtract))
                done(dec_sub, nc.vector.tensor_tensor(dec, dec, decneg.unsqueeze(1).to_broadcast([P, H, P]), ALU.add))
                dve.wait_ge(dec_exp.sem, t + 1)
                for i in range(4):
                    pair = bank[4 + i].ap().rearrange("p (h w n) -> p h w n", h=2, w=2)
                    first = 4 * (i % 2) + i // 2
                    hs = slice(first, first + 3, 2)
                    step(nc.vector.tensor_tensor(LT[:, hs, :], pair[:, :, 0, :], dec[:, hs, :], ALU.mult))
                    ins = nc.vector.tensor_tensor(dec[:, hs, :], pair[:, :, 1, :], dec[:, hs, :], ALU.mult)
                    done(lt_done, ins) if i == 3 else step(ins)
                for l in range(NL):
                    for hb in range(2):
                        hs = slice(4 * hb, 4 * hb + 4)
                        if l:
                            dve.wait_ge(p1_mm.sem, 2 * (NL * t + l - 1) + hb + 1)
                        done(lm_done, nc.vector.tensor_tensor(Lm[:, hs, :], LT[:, hs, :], lvl[:, l, :].unsqueeze(1).to_broadcast([P, 4, P]), ALU.mult))
                    for hb in range(2):
                        hs = slice(4 * hb, 4 * hb + 4)
                        i4 = ident.unsqueeze(1).to_broadcast([P, 4, P])
                        if l == 0:
                            done(u_sb, nc.vector.tensor_tensor(Um[:, hs, :], i4, Lm[:, hs, :], ALU.subtract))
                            dve.wait_ge(p1_mm.sem, 2 * NL * t + hb + 1)
                            done(t_sb, nc.vector.tensor_tensor(Tm[:, hs, :], i4, bank[hb].ap().rearrange("p (h n) -> p h n", h=4), ALU.subtract))
                        else:
                            dve.wait_ge(q_mm.sem, 2 * ((NL - 1) * t + l - 1) + hb + 1)
                            done(u_sb, nc.vector.tensor_tensor(Um[:, hs, :], Um[:, hs, :], bank[2 + hb].ap().rearrange("p (h n) -> p h n", h=4), ALU.subtract))
                            if l < NL - 1:
                                dve.wait_ge(t_mm.sem, 2 * ((NL - 2) * t + l - 1) + hb + 1)
                                done(t_sb, nc.vector.tensor_copy(Tm[:, hs, :], bank[4 + hb].ap().rearrange("p (h n) -> p h n", h=4)))
                dve.wait_ge(w_mm.sem, t + 1)
                done(w1_sb, nc.vector.tensor_copy(w1, bank[6].ap()))
                for ch in range(2):
                    n = 2 * t + ch
                    k = slice(64 * ch, 64 * ch + 64)
                    dve.wait_ge(un_mm.sem, n + 1)
                    for par in range(2):
                        done(un_sb, nc.vector.tensor_tensor(hd(u[k])[:, par::2, :], hd(bank[3 * par][k, :])[:, 0:CW, :], hd(w1[k])[:, par::2, :], ALU.add))
                    dve.wait_ge(od_mm.sem, n + 1)
                    step(nc.vector.tensor_tensor(S, S, glast[:, ch, t, :].unsqueeze(2).to_broadcast([P, CW, HD]), ALU.mult))
                    done(st_sb2, nc.vector.tensor_tensor(S, S, bank[2][:, 0:256].rearrange("p (c d) -> p c d", c=CW), ALU.add))
                for par in range(2):
                    step(nc.vector.tensor_copy(q[:, par::2, :], hd(bank[1 + 3 * par][:, :])[:, 0:CW, :]))
                done(o_sb, nc.vector.tensor_tensor(qkv_tm[:, t, 0:W], qkv_tm[:, t, 0:W], bank[5].ap(), ALU.add))

        @block.scalar
        def _(act):
            step = chained(act, ach)
            for t in range(PT):
                act.wait_ge(tr_mm.sem, t + 1)
                if t:
                    act.wait_ge(od_mm.sem, 2 * t)
                for i in range(4):
                    ins = nc.scalar.copy(trT[:, i], bank[i].ap().rearrange("p (c n) -> p c n", c=CW))
                    tr_sb.inc(ins) if i == 3 else step(ins)
                act.wait_ge(dec_sub.sem, t + 1)
                dec_exp.inc(nc.scalar.activation(dec, dec, ACT.Exp))
                for l in range(1, NL):
                    for hb in range(2):
                        act.wait_ge(p1_mm.sem, 2 * (NL * t + l) + hb + 1)
                        p1_sb.inc(nc.scalar.copy(P1[:, 4 * hb:4 * hb + 4, :], bank[hb].ap().rearrange("p (h n) -> p h n", h=4)))
                act.wait_ge(w_mm.sem, t + 1)
                w2_sb.inc(nc.scalar.mul(nw2T, bank[7].ap().rearrange("p (c n) -> p c n", c=CW), -1.0))

        @block.sync
        def _(sp):
            st = A["state_ssm"][0].rearrange("b h k v -> (b h) k v")
            sp.wait_ge(rows_out.sem, rows_out.n)
            for half in range(2):
                r = slice(64 * half, 64 * half + 64)
                in_load.inc(sp.dma_start(sS[r], st[:, :, 32 * half:32 * half + 32]), 16)
                in_load.inc(sp.dma_start(sx[r], scr.rearrange("b h t i d -> (b h) t i d")), 16)
                in_load.inc(sp.dma_start(sab[r], scr_ab.rearrange("b h t c -> (b h) t c")), 16)
            sp.wait_ge(srec.sem, 1)
            out = A["ssm_sample"][0].rearrange("b h k v -> (b h) k v")
            for half in range(2):
                r = slice(64 * half, 64 * half + 64)
                stored.inc(sp.dma_start(out[:, :, 32 * half:32 * half + 32], sS[r]), 16)
                so_back.inc(sp.dma_start(scr_o.rearrange("b h t d -> (b h) t d")[:, :, 32 * half:32 * half + 32], so[r]), 16)
            sp.wait_ge(so_back.sem, 32)
            for b in range(DB):
                so_back.inc(sp.dma_start(qkv_tm[DS * b:DS * b + DS, PT, 0:W].rearrange("p (h d) -> p h d", h=H),
                                         scr_o[b].rearrange("h t d -> t h d")), 16)
            sp.wait_ge(st_sb2.sem, 2 * PT)
            sv4 = A["ssm_prompt"][0, 0].rearrange("(c two) k v -> two k c v", two=2)
            for par in range(2):
                stored.inc(sp.dma_start(sv4[par], S[64 * par:64 * par + 64]), 16)
            sp.wait_ge(stored.sem, stored.n)

        @block.gpsimd
        def _(pool):
            step = chained(pool, gch)
            pool.wait_ge(in_load.sem, 96)
            for half in range(2):
                r = slice(64 * half, 64 * half + 64)
                step(nc.gpsimd.tensor_copy(sv[r], sx[r, :, 2, 32 * half:32 * half + 32]))
            step(nc.gpsimd.tensor_scalar(snab, sab[:, :, 1], -1.0, None, ALU.mult))
            over_v = lambda x: x.unsqueeze(2).to_broadcast([P, HD, 32])
            by_v = stmp.rearrange("p k v -> p v k")
            TT, TS = nc.gpsimd.tensor_tensor, nc.gpsimd.tensor_scalar
            def sum_keys(out):
                n = HD // 2
                while n >= 1:
                    dst = stmp[:, 0:n, :] if n > 1 else out.unsqueeze(1)
                    step(TT(dst, stmp[:, 0:n, :], stmp[:, n:2 * n, :], ALU.add))
                    n //= 2
            for t in range(DS):
                kt, qt = sx[:, t, 1, :], sx[:, t, 0, :]
                step(TT(stmp, sS, over_v(kt), ALU.mult))
                sum_keys(skv)
                step(TS(skv, skv, snab[:, t:t + 1], None, ALU.mult))
                step(TT(skv, skv, sv[:, t, :], ALU.add))
                step(TS(skv, skv, sab[:, t, 0:1], None, ALU.mult))
                step(TT(stmp, over_v(kt), skv.unsqueeze(1).to_broadcast([P, HD, 32]), ALU.mult))
                step(TS(sS, sS, sab[:, t, 1:2], None, ALU.mult))
                step(TT(sS, sS, stmp, ALU.add))
                step(TT(stmp, sS, over_v(qt), ALU.mult))
                sum_keys(so[:, t, :])
            srec.inc(nc.gpsimd.tensor_copy(skv, so[:, 0, :]))

    sqt = at(T2 + 512, W)
    ro = at(T2 + 1600, NT, H)
    on = [at(T2 + 1700 + 512 * i, W) for i in range(2)]
    ro_sum, ro_root, on_done, onT_mm, onT_sb = (Tick(nc, n) for n in (
        "out_squares_summed", "out_norms_rooted", "gated_out_done", "gated_outT_in_psum", "gated_outT_copied"))
    with nc.Block() as block:
        @block.vector
        def _(dve):
            step = chained(dve, vch)
            hd = lambda v: v.rearrange("p (h d) -> p h d", h=H)
            dve.wait_ge(so_back.sem, so_back.n)
            for t in range(NT):
                x = qkv_tm[:, t, 0:W]
                step(nc.vector.tensor_tensor(sqt, x, x, ALU.mult))
                step(nc.vector.tensor_reduce(ro[:, t, :], hd(sqt), AX.X, ALU.add))
            done(ro_sum, nc.vector.tensor_scalar(ro, ro, 1.0 / HD, RMS_EPS, ALU.mult, ALU.add))
            dve.wait_ge(ro_root.sem, 1)
            step(nc.vector.reciprocal(ro, ro))
            for t in range(NT):
                if t >= 2:
                    dve.wait_ge(onT_mm.sem, t - 1)
                o = on[t % 2]
                step(nc.vector.tensor_tensor(hd(o), hd(qkv_tm[:, t, 0:W]), ro[:, t, :].unsqueeze(2).to_broadcast([P, H, HD]), ALU.mult))
                step(nc.vector.tensor_tensor(hd(o), hd(o), normg.unsqueeze(1).to_broadcast([P, H, HD]), ALU.mult))
                done(on_done, nc.vector.tensor_tensor(o, o, z_tm[:, t, :], ALU.mult))

        @block.tensor
        def _(pe):
            for t in range(NT):
                n = TOKS[t]
                pe.wait_ge(on_done.sem, t + 1)
                if t >= 2:
                    pe.wait_ge(onT_sb.sem, t - 1)
                for cc in range(CW):
                    mm = nc.tensor.transpose(bank[t % 2][:, cc * n:(cc + 1) * n], on[t % 2][0:n, cc * P:(cc + 1) * P], ident[0:n, 0:n])
                onT_mm.inc(mm)

        @block.scalar
        def _(act):
            act.wait_ge(ro_sum.sem, 1)
            ro_root.inc(nc.scalar.activation(ro, ro, ACT.Sqrt))
            for t in range(NT):
                n = TOKS[t]
                act.wait_ge(onT_mm.sem, t + 1)
                onT_sb.inc(nc.scalar.copy(oTa[:, :, t * P:t * P + n], bank[t % 2][:, 0:CW * n].rearrange("p (c n) -> p c n", c=CW)))

        @block.sync
        def _(sp):
            send_until(sp, GATES + 3)

    next_phases()

    wba, wbb = at(T1, CW, D), at(T1 + 4096, CW, D)
    mod4 = at(T1 + 8192, 4 * D, p=DB + 1)
    mT = at(T2, KD, TOK)
    sga, sgb, ta, tb = (at(T2 + 4352 + TOK * i, TOK) for i in range(4))
    wb_load, b4_load = Tick(nc, "branch_weights_loaded"), Tick(nc, "mod_bias_loaded")
    ga_mm, gb_mm, ya_mm, yb_mm = (Tick(nc, n) for n in ("ga_product", "gb_product", "branch_a_product", "branch_b_product"))
    ga_sb, gb_sb, ta_done, tb_done = (Tick(nc, n) for n in ("ga_sigmoid", "gb_sigmoid", "branch_a_gated", "branch_b_gated"))
    with nc.Block() as block:
        @block.tensor
        def _(pe):
            for m in range(KD):
                for w_i, tick, free, rhs, b0 in ((GATES + 2 * (m // 4), ga_mm, ga_sb, None, 0), (0, ya_mm, ta_done, oTa, 2),
                                                 (GATES + 1 + 2 * (m // 4), gb_mm, gb_sb, None, 4), (1, yb_mm, tb_done, oTb, 6)):
                    if m:
                        pe.wait_ge(free.sem, m)
                    if rhs is None:
                        tick.inc(feature_major(arrived(pe, w_i), m % 4, hT, bank[b0:b0 + 2]))
                        if m % 4 == 3:
                            read_by(w_i, tick)
                    else:
                        pe.wait_ge(wb_load.sem, 32)
                        tick.inc(feature_major((wba, wbb)[w_i], m, rhs, bank[b0:b0 + 2], CW))

        @block.sync
        def _(sp):
            send_until(sp, OUTP + 3)

        @block.scalar
        def _(act):
            step = chained(act, ach)
            wb_load.inc(act.dma_start(wba, A["w_branch_a"][0].rearrange("(k p) n -> p k n", p=P)), 16)
            wb_load.inc(act.dma_start(wbb, A["w_branch_b"][0].rearrange("(k p) n -> p k n", p=P)), 16)
            b4_load.inc(act.dma_start(mod4, A["b_ada"][0:1, 2 * D:6 * D].broadcast_to([DB + 1, 4 * D])), 16)
            for m in range(KD):
                for tick, out, s, b0, read in ((ga_mm, ga_sb, sga, 0, ta_done), (gb_mm, gb_sb, sgb, 4, tb_done)):
                    act.wait_ge(tick.sem, m + 1)
                    if m:
                        act.wait_ge(read.sem, m)
                    step(nc.scalar.activation(s[:, 0:HALF], bank[b0][:, 0:HALF], ACT.Sigmoid))
                    out.inc(nc.scalar.activation(s[:, HALF:TOK], bank[b0 + 1][:, 0:HALF], ACT.Sigmoid))

        @block.vector
        def _(dve):
            step = chained(dve, vch)
            for m in range(KD):
                for y, s_sb, out, s, b0, tick in ((ya_mm, ga_sb, ta, sga, 2, ta_done), (yb_mm, gb_sb, tb, sgb, 6, tb_done)):
                    dve.wait_ge(y.sem, m + 1)
                    dve.wait_ge(s_sb.sem, m + 1)
                    step(nc.vector.tensor_tensor(out[:, 0:HALF], bank[b0][:, 0:HALF], s[:, 0:HALF], ALU.mult))
                    done(tick, nc.vector.tensor_tensor(out[:, HALF:TOK], bank[b0 + 1][:, 0:HALF], s[:, HALF:TOK], ALU.mult))
                step(nc.vector.tensor_tensor(mT[:, m, :], ta, tb, ALU.add))

    gtb = at(T1, 2, D)
    lng, lnb = at(T1 + 2048, D), at(T1 + 3072, D)
    res = at(T2 + 4352, D)
    stat = at(T2 + 5400, 16)
    ln_load, gt_mm, gt_add, gtb_mm, gtb_sb = (Tick(nc, n) for n in (
        "ln_params_loaded", "gate_product", "gate_added", "gate_broadcast", "gate_broadcast_copied"))
    wo_mm, wo_read, var_done, root_done, x1_done = (Tick(nc, n) for n in (
        "out_projection", "out_projection_read", "variance_done", "deviation_done", "x1_done"))

    def residual(y, gates, x, n, read):
        step = chained(nc.vector, vch)
        for i in range(2):
            cols = slice(512 * i, 512 * i + 512)
            ins = nc.vector.tensor_tensor(res[0:n, cols], y[i], gates[0:n, cols], ALU.mult)
            done(read, ins) if i else step(ins)
        step(nc.vector.scalar_tensor_tensor(res[0:n], x[0:n], ALPHA, res[0:n], ALU.mult, ALU.add))

    def layernorm(dve, n, out, g, b, last):
        step = chained(dve, vch)
        for i in range(2):
            step(nc.vector.bn_stats(stat[0:n, 6 * i:6 * i + 6], res[0:n, 512 * i:512 * i + 512]))
        step(nc.vector.bn_aggr(stat[0:n, 12:14], stat[0:n, 0:12]))
        done(var_done, nc.vector.tensor_scalar(stat[0:n, 13:14], stat[0:n, 13:14], LN_EPS, None, ALU.add))
        dve.wait_ge(root_done.sem, var_done.n)
        step(nc.vector.reciprocal(stat[0:n, 13:14], stat[0:n, 13:14]))
        step(nc.vector.tensor_scalar(res[0:n], res[0:n], stat[0:n, 12:13], stat[0:n, 13:14], ALU.subtract, ALU.mult))
        step(nc.vector.tensor_tensor(res[0:n], res[0:n], g[0:n], ALU.mult))
        done(last, nc.vector.tensor_tensor(out, res[0:n], b[0:n], ALU.add))

    def roots(act):
        for t in range(NT):
            act.wait_ge(var_done.sem, root_done.n + 1)
            v = stat[0:TOKS[t], 13:14]
            root_done.inc(nc.scalar.activation(v, v, ACT.Sqrt))

    def mod_chunks(pe, first, n, tick, banks):
        for i in range(n):
            w = arrived(pe, first + i)
            for k in range(KD):
                mm = nc.tensor.matmul(banks[i][0:DB + 1, :], cT[:, k, :], w[:, k, :], start=k == 0, stop=k == KD - 1)
            tick.inc(mm)
            read_by(first + i, tick)

    with nc.Block() as block:
        @block.tensor
        def _(pe):
            mod_chunks(pe, OUTP, 2, gt_mm, bank[4:6])
            pe.wait_ge(gt_add.sem, 2)
            for i, (sel, n) in enumerate(((selP, P), (selS, NS_TOK))):
                for half in range(2):
                    mm = nc.tensor.matmul(bank[4 + 2 * i + half][0:n, :], sel, mod4[:, 512 * half:512 * half + 512], start=True, stop=True)
            gtb_mm.inc(mm)
            for t in range(NT):
                if t >= 2:
                    pe.wait_ge(wo_read.sem, t - 1)
                for half in range(2):
                    w = arrived(pe, OUTP + 2 + half)
                    mm = token_major(bank[2 * (t % 2) + half][0:TOKS[t], :], t, mT, w, slice(0, 512))
                wo_mm.inc(mm)
            read_by(OUTP + 2, wo_mm)
            read_by(OUTP + 3, wo_mm)

        @block.sync
        def _(sp):
            ln_load.inc(sp.dma_start(lng, A["ln1_g"].broadcast_to([P, D])), 16)
            ln_load.inc(sp.dma_start(lnb, A["ln1_b"].broadcast_to([P, D])), 16)
            send_until(sp, OUTP + 7)

        @block.scalar
        def _(act):
            act.wait_ge(gtb_mm.sem, 1)
            for i, n in enumerate((P, NS_TOK)):
                for half in range(2):
                    gtb_sb.inc(nc.scalar.copy(gtb[0:n, i, 512 * half:512 * half + 512], bank[4 + 2 * i + half][0:n, :]))
            roots(act)

        @block.vector
        def _(dve):
            dve.wait_ge(b4_load.sem, 16)
            for i in range(2):
                dve.wait_ge(gt_mm.sem, i + 1)
                m = mod4[:, 512 * i:512 * i + 512]
                done(gt_add, nc.vector.tensor_tensor(m, bank[4 + i][0:DB + 1, :], m, ALU.add))
            dve.wait_ge(gtb_sb.sem, 4)
            dve.wait_ge(ln_load.sem, 32)
            for t in range(NT):
                n = TOKS[t]
                dve.wait_ge(wo_mm.sem, t + 1)
                a = 2 * (t % 2)
                residual([bank[a][0:n, :], bank[a + 1][0:n, :]], gtb[:, t // PT], x_tm[:, t], n, wo_read)
                layernorm(dve, n, x_tm[0:n, t, :], lng, lnb, x1_done)

    h2 = at(T1, NT, D)
    gt2b = at(X0 + 9472, 2, D)
    wr, rb = at(T2, KD, E), at(T2 + 512, E)
    sig = at(T2 + 576, NT, E)
    filler = at(T2 + 900, NU, 2)
    zero = at(T2 + 1108, D)
    iotaE, iotap, tokf = at(T2 + 2132, E), at(T2 + 2196, 1), at(T2 + 2197, NT)
    ltg = at(T2 + 2202, 8, 8)
    h2_d = nc.dram_tensor("h2_rows", (TOK + DUMMY, D), F32).ap()
    acc_d = [nc.dram_tensor(f"ffn_rows{i}", (TOK + DUMMY, D), F32).ap() for i in range(2)]
    list_d = nc.dram_tensor("slot_list", (NU * P, 2), F32).ap()
    table_d = nc.dram_tensor("overflow_table", (OVER + 1, 1), I32).ap()
    m2_mm, m2_add, b2_mm, h2_done, h2T_mm, h2T_sb = (Tick(nc, n) for n in (
        "mod2_product", "mod2_added", "mod2_broadcast", "h2_done", "h2T_in_psum", "h2T_copied"))
    g2_mm, g2_sb, lg_mm, sig_done, fill_done = (Tick(nc, n) for n in (
        "gate2_broadcast", "gate2_copied", "logits", "scores_sigmoid", "fillers_done"))
    r_load, side_store, h2_store = Tick(nc, "router_loaded"), Tick(nc, "fillers_stored"), Tick(nc, "h2_stored")
    MOD2 = OUTP + 4
    with nc.Block() as block:
        @block.tensor
        def _(pe):
            mod_chunks(pe, MOD2, 4, m2_mm, bank[0:4])
            pe.wait_ge(m2_add.sem, 4)
            for kind, sel, n in ((0, selP, P), (1, selS, NS_TOK)):
                if kind:
                    pe.wait_ge(h2_done.sem, PT)
                for i in range(4):
                    mm = nc.tensor.matmul(bank[i][0:n, :], sel, mod4[:, D + 512 * i:D + 512 * i + 512], start=True, stop=True)
                b2_mm.inc(mm)
                for t in (range(PT) if not kind else (PT,)):
                    pe.wait_ge(h2_done.sem, t + 1)
                    for half in range(2):
                        j = 2 * t + half
                        if j >= 4:
                            pe.wait_ge(h2T_sb.sem, j - 3)
                        for k in range(4):
                            kk = 4 * half + k
                            mm = nc.tensor.transpose(bank[4 + j % 4][:, k * n:(k + 1) * n], h2[0:n, t, kk * P:(kk + 1) * P], ident[0:n, 0:n])
                        h2T_mm.inc(mm)
            pe.wait_ge(h2T_sb.sem, 2 * NT)
            pe.wait_ge(r_load.sem, 32)
            for t in range(NT):
                mm = token_major(bank[4][0:TOKS[t], E * t:E * t + E], t, hT, wr, slice(0, E))
            lg_mm.inc(mm)
            pe.wait_ge(h2_done.sem, NT)
            mod_chunks(pe, MOD2 + 4, 2, m2_mm, bank[5:7])
            pe.wait_ge(m2_add.sem, 6)
            for i, (sel, n) in enumerate(((selP, P), (selS, NS_TOK))):
                for half in range(2):
                    mm = nc.tensor.matmul(bank[2 * i + half][0:n, :], sel, mod4[:, 3 * D + 512 * half:3 * D + 512 * half + 512], start=True, stop=True)
            g2_mm.inc(mm)

        @block.sync
        def _(sp):
            r_load.inc(sp.dma_start(wr, A["w_router"][0].rearrange("(p k) n -> p k n", p=P)), 16)
            r_load.inc(sp.dma_start(rb, A["router_bias"].broadcast_to([P, E])), 16)
            send_until(sp, len(stream))
            sp.wait_ge(fill_done.sem, 1)
            side_store.inc(sp.dma_start(list_d.rearrange("(p u) c -> p (u c)", u=NU), filler.rearrange("p u c -> p (u c)")), 16)
            side_store.inc(sp.dma_start(h2_d[TOK:TOK + DUMMY, :], zero), 16)
            side_store.inc(sp.dma_start(acc_d[0][TOK:TOK + DUMMY, :], zero), 16)
            for a in range(0, SEQ, P):
                side_store.inc(sp.dma_start(acc_d[1][a:a + P, :], zero), 16)
            side_store.inc(sp.dma_start(acc_d[1][SEQ:TOK, :], zero[0:NS_TOK]), 16)
            side_store.inc(sp.dma_start(acc_d[1][TOK:TOK + DUMMY, :], zero), 16)
            sp.wait_ge(h2_done.sem, NT)
            h2_store.inc(sp.dma_start(h2_d[0:SEQ, :].rearrange("(t p) d -> p t d", p=P), h2[:, 0:PT, :]), 16)
            h2_store.inc(sp.dma_start(h2_d[SEQ:TOK, :], h2[0:NS_TOK, PT, :]), 16)
            sp.wait_ge(h2_store.sem, 32)
            sp.wait_ge(side_store.sem, side_store.n)

        @block.gpsimd
        def _(pool):
            step = chained(pool, gch)
            fl = dict(allow_small_or_imprecise_dtypes=True)
            step(pool.iota(iotaE, pattern=[[1, E]], base=0, channel_multiplier=0, **fl))
            step(pool.iota(iotap, pattern=[[1, 1]], base=0, channel_multiplier=1, **fl))
            step(pool.iota(tokf, pattern=[[P, NT]], base=0, channel_multiplier=1, **fl))
            step(pool.memset(ltg, 1.0))
            step(pool.affine_select(out=ltg, in_=ltg, compare_op=ALU.is_ge, fill=0.0, base=-1, pattern=[[1, 8], [-1, 8]], channel_multiplier=0))
            step(pool.memset(filler, 0.0))
            step(pool.iota(filler[:, :, 0], pattern=[[0, NU]], base=TOK, channel_multiplier=1, **fl))
            step(pool.memset(sig, 0.5))
            fill_done.inc(pool.memset(zero, 0.0))

        @block.scalar
        def _(act):
            for t in range(NT):
                n = TOKS[t]
                for half in range(2):
                    act.wait_ge(h2T_mm.sem, 2 * t + half + 1)
                    src = bank[4 + (2 * t + half) % 4][:, 0:4 * n].rearrange("p (k n) -> p k n", k=4)
                    h2T_sb.inc(nc.scalar.copy(hT[:, 4 * half:4 * half + 4, t * P:t * P + n], src))
            act.wait_ge(lg_mm.sem, 1)
            act.wait_ge(fill_done.sem, 1)
            sig_done.inc(nc.scalar.activation(sig[:, 0:PT, :], bank[4][:, 0:E * PT].rearrange("p (t e) -> p t e", t=PT), ACT.Sigmoid))
            sig_done.inc(nc.scalar.activation(sig[0:NS_TOK, PT, :], bank[4][0:NS_TOK, E * PT:E * NT], ACT.Sigmoid))
            act.wait_ge(g2_mm.sem, 1)
            for i, n in enumerate((P, NS_TOK)):
                for half in range(2):
                    g2_sb.inc(nc.scalar.copy(gt2b[0:n, i, 512 * half:512 * half + 512], bank[2 * i + half][0:n, :]))

        @block.vector
        def _(dve):
            step = chained(dve, vch)
            for i in range(4):
                dve.wait_ge(m2_mm.sem, i + 1)
                m = mod4[:, D + 512 * i:D + 512 * i + 512]
                done(m2_add, nc.vector.tensor_tensor(m, bank[i][0:DB + 1, :], m, ALU.add))
            for t in range(NT):
                n = TOKS[t]
                dve.wait_ge(b2_mm.sem, 1 + t // PT)
                for i in range(2):
                    rows_of = lambda v: v.rearrange("p (f k) -> p f k", k=KD)
                    out = h2[0:n, t, :].rearrange("p (k f) -> p f k", k=KD)[:, 64 * i:64 * i + 64, :]
                    step(nc.vector.scalar_tensor_tensor(out, rows_of(bank[2 + i][0:n, :]), 1.0, rows_of(x_tm[0:n, t, 512 * i:512 * i + 512]), ALU.add, ALU.mult))
                    ins = nc.vector.tensor_tensor(out, out, rows_of(bank[i][0:n, :]), ALU.add)
                    done(h2_done, ins) if i else step(ins)
            for i in range(2):
                dve.wait_ge(m2_mm.sem, 5 + i)
                m = mod4[:, 3 * D + 512 * i:3 * D + 512 * i + 512]
                done(m2_add, nc.vector.tensor_tensor(m, bank[5 + i][0:DB + 1, :], m, ALU.add))

    def weights(i):
        return at(UW * i, KD, FF), at(UW * i + 2048, KD, FF), at(UW * i + 4096, 2, D)

    def load_expert(sp, i, tick, *of):
        for dst, src in zip(weights(i), of):
            tick.inc(sp.dma_start(dst, src.rearrange("(p k) n -> p k n", p=P)), 16)

    r0 = T2 + 2300
    sbias, msk, pos, fl_, selm = (at(r0 + 320 * i, NT, E) for i in range(5))
    addr, scr5 = at(r0 + 1600, NT, E), at(r0 + 1920, NT, E)
    m8 = at(r0 + 1920, NT, 8, 8)
    gsc, rank, eqm = at(r0 + 2240, NT, 8), at(r0 + 2280, NT, 8), at(r0 + 2320, NT, 8, 8)
    v8, idx8, idxf = at(r0 + 2640, NT, 8), at(r0 + 2680, NT, 8, dt=U32), at(r0 + 2720, NT, 8)
    adf, adi, sk = at(r0 + 2760, NT, 8), at(r0 + 2800, NT, 8, dt=U32), at(r0 + 2840, NT, 8)
    entry = at(r0 + 2880, NT, 8, 2)
    over, cum, base = at(r0 + 2960, E), at(r0 + 3024, E), at(r0 + 3088, E)
    wsum = at(r0 + 3152, NT)
    tabf, tabi = at(r0 + 3158, 1), at(r0 + 3159, 1, dt=I32)
    novi, junk = at(r0 + 3160, 1, dt=I32), at(r0 + 3164, E)
    lists = at(r0 + 3232, NU, 2)
    shA, shT, shY = at(X0 + 11520, 2, FF), at(X0 + 12032, 2, P), at(X0 + 12544, 2, 512)
    sh_u = at(X0 + 13568, FF)
    wl = [Tick(nc, f"expert_loaded{i}") for i in range(RING)]
    sel_done, pos_mm, ent_done, tab_done = (Tick(nc, n) for n in ("choice_done", "positions", "entries_done", "table_done"))
    shw, sg_mm, sg_sb, sg_act, sA, sT_mm, sT_sb, sd_mm, sd_sb, sh_out = (Tick(nc, n) for n in (
        "shared_loaded", "shared_up", "shared_up_copied", "shared_silu", "shared_hidden", "shared_hiddenT_in_psum",
        "shared_hiddenT_copied", "shared_down", "shared_copied", "shared_stored"))
    scat, tab_out, lists_in = Tick(nc, "entries_scattered"), Tick(nc, "table_stored"), Tick(nc, "lists_loaded")

    with nc.Block() as block:
        @block.sync
        def _(sp):
            load_expert(sp, 3, shw, A["ws_gate"][0], A["ws_up"][0], A["ws_down"][0])
            for i in range(3):
                load_expert(sp, i, wl[i], A["w_gate"][0, i], A["w_up"][0, i], A["w_down"][0, i])
            for t in range(NT):
                sp.wait_ge(sd_sb.sem, 2 * t + 2)
                sh_out.inc(sp.dma_start(acc_d[0][P * t:P * t + TOKS[t], :], shY[0:TOKS[t]].rearrange("p a n -> p (a n)")), 16)
            sp.wait_ge(sh_out.sem, 16 * NT)

        @block.tensor
        def _(pe):
            both, dn = at(UW * 3, 2, KD, FF), weights(3)[2]
            pe.wait_ge(shw.sem, 48)
            def up(t):
                if t:
                    pe.wait_ge(sg_act.sem, t)
                    pe.wait_ge(sg_sb.sem, t)
                n = TOKS[t]
                out = bank[0][0:n, :].rearrange("p (a n) -> p a n", a=2)
                for k in range(KD):
                    mm = nc.tensor.matmul(out, hT[:, k, t * P:t * P + n], both[:, :, k, :], start=k == 0, stop=k == KD - 1)
                sg_mm.inc(mm)

            def down(t):
                n = TOKS[t]
                pe.wait_ge(sA.sem, t + 1)
                if t:
                    pe.wait_ge(sT_sb.sem, t)
                for k in range(2):
                    mm = nc.tensor.transpose(bank[1][:, k * n:(k + 1) * n], shA[0:n, 0, :].rearrange("p (f k) -> p k f", k=2)[:, k, :], ident[0:n, 0:n])
                sT_mm.inc(mm)
                pe.wait_ge(sT_sb.sem, t + 1)
                if t:
                    pe.wait_ge(sd_sb.sem, 2 * t)
                for half in range(2):
                    for k in range(2):
                        mm = nc.tensor.matmul(bank[2 + half][0:n, :], shT[:, k, 0:n], dn[:, k, 512 * half:512 * half + 512], start=k == 0, stop=k == 1)
                    sd_mm.inc(mm)
            for t in range(NT):
                up(t)
                if t == 1:
                    pe.wait_ge(sel_done.sem, NT + 1)
                    for i in range(NT):
                        for s in range(i + 1):
                            nc.tensor.matmul(bank[7][:, E * i:E * i + E], strictU if s == i else ones, selm[:, s, :], start=s == 0, stop=s == i)
                    for s in range(NT):
                        mm = nc.tensor.matmul(bank[7][:, E * NT:E * NT + E], ones, selm[:, s, :], start=s == 0, stop=s == NT - 1)
                    pos_mm.inc(mm)
                down(t)

        @block.scalar
        def _(act):
            for t in range(NT):
                n = TOKS[t]
                act.wait_ge(sg_mm.sem, t + 1)
                if t:
                    act.wait_ge(sT_mm.sem, t)
                sg_act.inc(nc.scalar.activation(shA[0:n, 1, :], bank[0][0:n, 0:FF], ACT.Silu))
                sg_sb.inc(nc.scalar.copy(sh_u[0:n], bank[0][0:n, FF:2 * FF]))
                act.wait_ge(sT_mm.sem, t + 1)
                if t:
                    act.wait_ge(sd_mm.sem, 2 * t)
                sT_sb.inc(nc.scalar.copy(shT[:, :, 0:n], bank[1][:, 0:2 * n].rearrange("p (k n) -> p k n", k=2)))
                for half in range(2):
                    act.wait_ge(sd_mm.sem, 2 * t + half + 1)
                    if t:
                        act.wait_ge(sh_out.sem, 16 * t)
                    sd_sb.inc(nc.scalar.copy(shY[0:n, half, :], bank[2 + half][0:n, :]))

        @block.gpsimd
        def _(pool):
            for t in range(NT):
                n = TOKS[t]
                pool.wait_ge(sg_act.sem, t + 1)
                pool.wait_ge(sg_sb.sem, t + 1)
                sA.inc(nc.gpsimd.tensor_tensor(shA[0:n, 0, :], shA[0:n, 1, :], sh_u[0:n], ALU.mult))
            for t in range(NT):
                n = TOKS[t]
                pool.wait_ge(ent_done.sem, t + 1)
                for k in range(TOPK):
                    scat.inc(nc.gpsimd.indirect_dma_start(out=list_d, out_offset=bass.IndirectOffsetOnAxis(ap=adi[0:n, t, k:k + 1], axis=0),
                                                          in_=entry[0:n, t, k, :], in_offset=None), 16)
            pool.wait_ge(tab_done.sem, 2)
            tab_out.inc(pool.dma_start(table_d[0:OVER, :], tabi[0:OVER]), 16)
            tab_out.inc(pool.dma_start(table_d[OVER:OVER + 1, :], novi[0:1]), 16)
            pool.wait_ge(scat.sem, scat.n)
            lists_in.inc(pool.dma_start(lists.rearrange("p u c -> p (u c)"), list_d.rearrange("(p u) c -> p (u c)", u=NU)), 16)
            pool.wait_ge(tab_out.sem, 32)
            pool.wait_ge(lists_in.sem, 16)

        @block.vector
        def _(dve):
            step = chained(dve, vch)
            TT, TS, STT = nc.vector.tensor_tensor, nc.vector.tensor_scalar, nc.vector.scalar_tensor_tensor
            tall = lambda v, *s: v.unsqueeze(1).to_broadcast([P, NT] + list(s))
            step(TT(sbias, sig, tall(rb, E), ALU.add))
            for t in range(NT):
                for g in range(8):
                    step(nc.vector.max(m8[:, t, g, :], sbias[:, t, 8 * g:8 * g + 8]))
            step(TT(gsc, m8[:, :, :, 0], m8[:, :, :, 1], ALU.add))
            other, own = gsc.unsqueeze(2).to_broadcast([P, NT, 8, 8]), gsc.unsqueeze(3).to_broadcast([P, NT, 8, 8])
            step(TT(eqm, other, own, ALU.is_equal))
            step(TT(eqm, eqm, tall(ltg, 8, 8), ALU.mult))
            step(TT(m8, other, own, ALU.is_gt))
            step(TT(eqm, eqm, m8, ALU.add))
            step(nc.vector.tensor_reduce(rank, eqm, AX.X, ALU.add))
            step(TS(rank, rank, float(TOPG), None, ALU.is_lt))
            step(TS(rank, rank, 1e30, 1e30, ALU.mult, ALU.subtract))
            g8 = lambda v: v.rearrange("p t (g e) -> p t g e", g=8)
            step(TT(g8(msk), g8(sbias), rank.unsqueeze(3).to_broadcast([P, NT, 8, 8]), ALU.add))
            for t in range(NT):
                step(nc.vector.max(v8[:, t, :], msk[:, t, :]))
                step(nc.vector.max_index(idx8[:, t, :], v8[:, t, :], msk[:, t, :]))
                step(nc.vector.match_replace(out=scr5[:, t, :], in_to_replace=v8[:, t, :], in_values=msk[:, t, :], imm_value=1e30))
                done(sel_done, TS(selm[:, t, :], scr5[:, t, :], 1e29, None, ALU.is_ge))
            step(nc.vector.memset(selm[NS_TOK:64, PT, :], 0.0))
            done(sel_done, nc.vector.memset(selm[64:P, PT, :], 0.0))
            step(nc.vector.tensor_copy(idxf, idx8))
            step(TT(scr5, sig, selm, ALU.mult))
            step(nc.vector.tensor_reduce(wsum, scr5, AX.X, ALU.add))
            step(TS(wsum, wsum, 1e-30, None, ALU.max))
            step(nc.vector.reciprocal(wsum, wsum))
            step(TS(wsum, wsum, ROUTED, None, ALU.mult))
            dve.wait_ge(pos_mm.sem, 1)
            step(nc.vector.tensor_copy(pos, bank[7][:, 0:E * NT].rearrange("p (t e) -> p t e", t=NT)))
            step(nc.vector.tensor_copy(base, bank[7][:, E * NT:E * NT + E]))
            step(TS(fl_, pos, float(P), None, ALU.is_ge))
            step(TS(over, base, float(P), None, ALU.is_gt))
            for j in range(2, TOK // P + 1):
                step(STT(fl_, pos, float(P * j), fl_, ALU.is_ge, ALU.add))
                step(STT(over, base, float(P * j), over, ALU.is_gt, ALU.add))
            step(nc.vector.memset(junk, 1.0))
            step(nc.vector.tensor_tensor_scan(cum, junk, over, 0.0, ALU.mult, ALU.add))
            step(TT(base, cum, over, ALU.subtract))
            step(TS(base, base, float(E - 1), None, ALU.add))
            step(TT(base, base, iotaE, ALU.subtract))
            step(STT(pos, fl_, -float(P), pos, ALU.mult, ALU.add))
            step(TS(scr5, fl_, 0.0, None, ALU.is_gt))
            step(TT(fl_, fl_, tall(base, E), ALU.add))
            step(TT(fl_, fl_, scr5, ALU.mult))
            step(TT(fl_, fl_, tall(iotaE, E), ALU.add))
            step(STT(addr, pos, float(NU), fl_, ALU.mult, ALU.add))
            step(nc.vector.tensor_copy(entry[:, :, :, 0], tokf.unsqueeze(2).to_broadcast([P, NT, 8])))
            for t in range(NT):
                for k in range(TOPK):
                    e = idxf[:, t, k:k + 1]
                    step(STT(junk, iotaE, e, addr[:, t, :], ALU.is_equal, ALU.mult, accum_out=adf[:, t, k:k + 1]))
                    step(STT(junk, iotaE, e, sig[:, t, :], ALU.is_equal, ALU.mult, accum_out=sk[:, t, k:k + 1]))
                step(nc.vector.tensor_copy(adi[:, t, :], adf[:, t, :]))
                done(ent_done, TS(entry[:, t, :, 1], sk[:, t, :], wsum[:, t:t + 1], None, ALU.mult))
            step(TS(junk, cum, iotap, None, ALU.is_le))
            step(nc.vector.tensor_reduce(tabf, junk, AX.X, ALU.add))
            step(TS(tabf, tabf, float(E - 1), None, ALU.min))
            done(tab_done, nc.vector.tensor_copy(tabi, tabf))
            step(TS(junk[:, 0:OVER // RING], iotaE[:, 0:OVER // RING], float(RING), cum[:, E - 1:E], ALU.mult, ALU.is_lt))
            step(nc.vector.tensor_reduce(tabf, junk[:, 0:OVER // RING], AX.X, ALU.add))
            step(TS(tabf, tabf, float(E // RING - 1), None, ALU.add))
            done(tab_done, nc.vector.tensor_copy(novi, tabf))

    Xg = [at(X0 + 5120 + D * i, D) for i in range(RING)]
    XT = [at(X0 + 11520 + D * i, KD, P) for i in range(2)]
    Yb = [at(X0 + 13568, D), at(X0 + 14592, D), at(T2, D), at(T2 + D, D)]
    hid = [at(T2 + 2048 + FF * i, FF) for i in range(2)]
    hidT = [at(T2 + 2560 + FF * i, 2, P) for i in range(2)]
    y0 = r0 + 3232 + 2 * NU
    gidx, sidx = ([at(y0 + RING * n + i, 1, dt=U32) for i in range(RING)] for n in range(2))
    gate = [at(y0 + 2 * RING + i, 1) for i in range(RING)]
    assert y0 + 3 * RING <= END and T2 + 3072 <= r0 + 3232
    g_ld = [Tick(nc, f"tokens_gathered{i}") for i in range(RING)]
    y_add = [Tick(nc, f"y_added{i}") for i in range(2)]
    xt_mm, xt_a, xt_v, gu_mm, silu_d, a_done, at_mm, at_sb2, d_mm, y_a, y_v, gi_rd, si_rd, gt_rd, turn = (Tick(nc, n) for n in (
        "xT_in_psum", "xT_copied_low", "xT_copied_high", "gate_up_product", "silu_done", "hidden_done", "hiddenT_in_psum",
        "hiddenT_copied", "down_product", "y_scaled_low", "y_scaled_high", "gather_index_read", "add_index_read",
        "gate_read", "pool_turn"))

    def at_least(eng, tick, i, c, scale=1):
        if isinstance(i, int) and 4 * i + c <= 0:
            return
        eng.wait_ge(tick.sem, i * (4 * scale) + c * scale)

    def added(eng, i, j, before):
        c = j // 2 + 1 - before // 2
        if isinstance(i, int) and 2 * i + c <= 0:
            return
        eng.wait_ge(y_add[j % 2].sem, i * 32 + 16 * c)

    def unit_after(i, j, n):
        return (i, j + n) if j + n < RING else (i + 1, j + n - RING)

    def unit_before(i, j):
        return (i, j - 1) if j else (i - 1, RING - 1)

    NB = E // RING
    NO = OVER // RING

    def run(eng, lead_in, step, lead_out):
        lead_in()
        for j in range(RING):
            step(0, j)
        with eng.Fori(1, NB) as i:
            for j in range(RING):
                step(i, j)
        last = eng.value_load(table_d[OVER:OVER + 1, :], min_val=NB - 1, max_val=NB - 1 + NO)
        with eng.Fori(NB, NB + NO) as i:
            with eng.If(last > i - 1):
                for j in range(RING):
                    step(i, j)
        lead_out(last)

    with nc.Block() as block:
        @block.sync
        def _(sp):
            def load(i, j, e):
                at_least(sp, d_mm, i, j - 3)
                for name, dst in zip(("w_gate", "w_up", "w_down"), weights(j)):
                    src = A[name][0, e] if isinstance(e, int) else A[name][0, bass.ds(e, 1)].rearrange("a r n -> (a r) n")
                    sp.dma_start(dst, src.rearrange("(p k) n -> p k n", p=P)).then_inc(wl[j].sem, 16)
            load(0, 3, 3)
            with sp.Fori(1, NB) as i:
                for j in range(RING):
                    load(i, j, i * RING + j)
            last = sp.value_load(table_d[OVER:OVER + 1, :], min_val=NB - 1, max_val=NB - 1 + NO)
            with sp.Fori(0, NO) as i:
                with sp.If(last > i + (NB - 1)):
                    for j in range(RING):
                        e = sp.value_load(table_d[bass.ds(i * RING + j, 1), :], min_val=0, max_val=E - 1)
                        load(i + NB, j, e)

        @block.tensor
        def _(pe):
            def xT(i, j):
                pe.wait_ge(g_ld[j].sem, i * 16 + 16)
                at_least(pe, xt_a, i, j)
                at_least(pe, xt_v, i, j)
                for half in range(2):
                    for k in range(4):
                        kk = 4 * half + k
                        mm = nc.tensor.transpose(bank[half][:, k * P:(k + 1) * P], Xg[j][:, kk * P:(kk + 1) * P], ident)
                    mm.then_inc(xt_mm.sem, 1)

            def up(i, j):
                at_least(pe, xt_a, i, j + 1)
                at_least(pe, xt_v, i, j + 1)
                pe.wait_ge(wl[j].sem, i * 48 + 48)
                at_least(pe, a_done, i, j - 1)
                both = at(UW * j, 2, KD, FF)
                out = bank[2 + j % 2].ap().rearrange("p (a n) -> p a n", a=2)
                for k in range(KD):
                    mm = nc.tensor.matmul(out, XT[j % 2][:, k, :], both[:, :, k, :], start=k == 0, stop=k == KD - 1)
                mm.then_inc(gu_mm.sem, 1)

            def hiddenT(i, j):
                at_least(pe, a_done, i, j + 1)
                at_least(pe, at_sb2, i, j)
                for k in range(2):
                    mm = nc.tensor.transpose(bank[4][:, k * P:(k + 1) * P], hid[j % 2].rearrange("p (f k) -> p k f", k=2)[:, k, :], ident)
                mm.then_inc(at_mm.sem, 1)

            def down(i, j):
                at_least(pe, at_sb2, i, j + 1)
                at_least(pe, y_a, i, j)
                at_least(pe, y_v, i, j)
                for half in range(2):
                    for k in range(2):
                        mm = nc.tensor.matmul(bank[5 + half][:, :], hidT[j % 2][:, k, :], weights(j)[2][:, k, 512 * half:512 * half + 512],
                                              start=k == 0, stop=k == 1)
                mm.then_inc(d_mm.sem, 1)

            def step(i, j):
                first = isinstance(i, int) and i + j == 0
                if not first:
                    hiddenT(*unit_before(i, j))
                xT(*unit_after(i, j, 1))
                up(i, j)
                if not first:
                    down(*unit_before(i, j))

            def lead_out(last):
                hiddenT(last, RING - 1)
                down(last, RING - 1)
            run(pe, lambda: xT(0, 0), step, lead_out)

        @block.scalar
        def _(act):
            def xT_low(i, j):
                act.wait_ge(xt_mm.sem, i * 8 + 2 * j + 1)
                at_least(act, gu_mm, i, j - 1)
                nc.scalar.copy(XT[j % 2][:, 0:4, :], bank[0].ap().rearrange("p (k n) -> p k n", k=4)).then_inc(xt_a.sem, 1)

            def silu(i, j):
                at_least(act, gu_mm, i, j + 1)
                at_least(act, at_mm, i, j - 1)
                nc.scalar.activation(hid[j % 2], bank[2 + j % 2][:, 0:FF], ACT.Silu).then_inc(silu_d.sem, 1)

            def y_low(i, j):
                at_least(act, d_mm, i, j + 1)
                added(act, i, j, RING)
                at_least(act, gt_rd, i, j + 1)
                nc.scalar.mul(Yb[j][:, 0:512], bank[5][:, :], gate[j]).then_inc(y_a.sem, 1)

            def step(i, j):
                xT_low(*unit_after(i, j, 1))
                silu(i, j)
                if not (isinstance(i, int) and i + j == 0):
                    y_low(*unit_before(i, j))
            run(act, lambda: xT_low(0, 0), step, lambda last: y_low(last, RING - 1))

        @block.vector
        def _(dve):
            def xT_high(i, j):
                dve.wait_ge(xt_mm.sem, i * 8 + 2 * j + 2)
                at_least(dve, gu_mm, i, j - 1)
                nc.vector.tensor_copy(XT[j % 2][:, 4:8, :], bank[1].ap().rearrange("p (k n) -> p k n", k=4)).then_inc(xt_v.sem, 1)

            def hidden(i, j):
                at_least(dve, silu_d, i, j + 1)
                h = hid[j % 2]
                nc.vector.tensor_tensor(h, h, bank[2 + j % 2][:, FF:2 * FF], ALU.mult).then_inc(a_done.sem, 1)

            def hiddenT(i, j):
                at_least(dve, at_mm, i, j + 1)
                at_least(dve, d_mm, i, j - 1)
                nc.vector.tensor_copy(hidT[j % 2], bank[4][:, 0:2 * P].rearrange("p (k n) -> p k n", k=2)).then_inc(at_sb2.sem, 1)

            def y_high(i, j):
                at_least(dve, d_mm, i, j + 1)
                added(dve, i, j, RING)
                at_least(dve, gt_rd, i, j + 1)
                nc.vector.tensor_scalar(Yb[j][:, 512:D], bank[6][:, :], gate[j], None, ALU.mult).then_inc(y_v.sem, 1)

            def step(i, j):
                first = isinstance(i, int) and i + j == 0
                if not first:
                    hiddenT(*unit_before(i, j))
                xT_high(*unit_after(i, j, 1))
                hidden(i, j)
                if not first:
                    y_high(*unit_before(i, j))

            def lead_out(last):
                hiddenT(last, RING - 1)
                y_high(last, RING - 1)
            run(dve, lambda: xT_high(0, 0), step, lead_out)

        @block.gpsimd
        def _(pool):
            def gather(i, j):
                at_least(pool, xt_mm, i, j - 3, 2)
                pool.sem_inc(turn.sem, 1)
                nc.gpsimd.tensor_copy(gidx[j], lists[:, bass.ds(i * 4 + j, 1), 0]).then_inc(gi_rd.sem, 1)
                at_least(pool, gi_rd, i, j + 1)
                pool.sem_inc(turn.sem, 1)
                nc.gpsimd.indirect_dma_start(out=Xg[j], out_offset=None, in_=h2_d,
                                             in_offset=bass.IndirectOffsetOnAxis(ap=gidx[j], axis=0)).then_inc(g_ld[j].sem, 16)

            def slots(i, j):
                at_least(pool, y_a, i, j - 3)
                at_least(pool, y_v, i, j - 3)
                added(pool, i, j, RING)
                pool.sem_inc(turn.sem, 1)
                nc.gpsimd.tensor_copy(gate[j], lists[:, bass.ds(i * 4 + j, 1), 1]).then_inc(gt_rd.sem, 1)
                nc.gpsimd.tensor_copy(sidx[j], lists[:, bass.ds(i * 4 + j, 1), 0]).then_inc(si_rd.sem, 1)

            def add(i, j):
                at_least(pool, si_rd, i, j + 1)
                at_least(pool, y_a, i, j + 1)
                at_least(pool, y_v, i, j + 1)
                added(pool, i, j, 2)
                pool.sem_inc(turn.sem, 1)
                nc.gpsimd.indirect_dma_start(out=acc_d[j % 2], out_offset=bass.IndirectOffsetOnAxis(ap=sidx[j], axis=0), in_=Yb[j],
                                             in_offset=None, compute_op=ALU.add).then_inc(y_add[j % 2].sem, 16)

            def lead_in():
                for j in range(RING - 1):
                    gather(0, j)

            def step(i, j):
                gather(*unit_after(i, j, RING - 1))
                slots(i, j)
                if not (isinstance(i, int) and i + j == 0):
                    add(*unit_before(i, j))

            def lead_out(last):
                add(last, RING - 1)
                for j in range(RING):
                    pool.wait_ge(g_ld[j].sem, last * 16 + (32 if j < RING - 1 else 16))
                for j in (RING - 2, RING - 1):
                    added(pool, last, j, 0)
            run(pool, lead_in, step, lead_out)

    ffn = [at(D * i, D) for i in range(NT)]
    ffn2 = [at(D * (2 * NT + 2 + i), D) for i in range(NT)]
    lng2, lnb2 = at(D * NT, D), at(D * NT + D, D)
    yout = [at(D * (NT + 2 + i), D) for i in range(NT)]
    l2_load, f_read, y_done = (Tick(nc, n) for n in ("ln2_loaded", "ffn_read", "y_done"))
    f_load = [Tick(nc, f"ffn_loaded{t}") for t in range(NT)]
    f_sum = Tick(nc, "ffn_summed")
    with nc.Block() as block:
        @block.sync
        def _(sp):
            l2_load.inc(sp.dma_start(lng2, A["ln2_g"].broadcast_to([P, D])), 16)
            l2_load.inc(sp.dma_start(lnb2, A["ln2_b"].broadcast_to([P, D])), 16)
            for t in range(NT):
                for dst, acc in zip((ffn, ffn2), acc_d):
                    f_load[t].inc(sp.dma_start(dst[t][0:TOKS[t]], acc[P * t:P * t + TOKS[t], :]), 16)
            for t in range(NT):
                sp.wait_ge(y_done.sem, t + 1)
                out = A["y_prompt"][0, P * t:P * t + P, :] if t < PT else A["y_sample"].rearrange("b t d -> (b t) d")
                stored.inc(sp.dma_start(out, yout[t][0:TOKS[t]]), 16)
            sp.wait_ge(stored.sem, stored.n)

        @block.scalar
        def _(act):
            roots(act)

        @block.vector
        def _(dve):
            dve.wait_ge(l2_load.sem, 32)
            for t in range(NT):
                n = TOKS[t]
                dve.wait_ge(f_load[t].sem, 32)
                done(f_sum, nc.vector.tensor_tensor(ffn[t][0:n], ffn[t][0:n], ffn2[t][0:n], ALU.add))
                residual([ffn[t][0:n, 0:512], ffn[t][0:n, 512:D]], gt2b[:, t // PT], x_tm[:, t], n, f_read)
                layernorm(dve, n, yout[t][0:n], lng2, lnb2, y_done)


IN = ["x_prompt", "x_sample", "c_prompt", "c_sample", "cache_k", "cache_v", "cache_logf", "state_ssm", "state_conv",
      "page_table", "w_ada", "b_ada", "w_in", "conv_w", "gdn_a_log", "gdn_dt_bias", "gdn_norm_g", "fox_f_bias",
      "w_branch_a", "w_branch_b", "w_out", "ln1_g", "ln1_b", "w_router", "router_bias", "w_gate", "w_up", "w_down",
      "ws_gate", "ws_up", "ws_down", "ln2_g", "ln2_b"]
OUT = dict(y_prompt=(1, SEQ, D), y_sample=(DB, DS, D), k_prompt=(1, 1, SEQ, H, HD), v_prompt=(1, 1, SEQ, H, HD),
           logf_prompt=(1, 1, SEQ, H), ssm_prompt=(1, 1, H, HD, HD), conv_prompt=(1, 1, CONV - 1, 3 * W),
           k_sample=(1, DB, DS, H, HD), v_sample=(1, DB, DS, H, HD), logf_sample=(1, DB, DS, H),
           ssm_sample=(1, DB, H, HD, HD), conv_sample=(1, DB, CONV - 1, 3 * W))


def kernel(**inputs):
    import concourse.bacc as bacc
    from concourse.bass_utils import run_bass_kernel_spmd

    nc = bacc.Bacc("TRN2", target_bir_lowering=False, num_devices=1)
    arrays, aps = {}, {}
    for name in IN:
        a = np.ascontiguousarray(inputs[name])
        arrays[f"in_{name}"] = a
        aps[name] = nc.dram_tensor(f"in_{name}", a.shape, mybir.dt.from_np(a.dtype), kind="ExternalInput").ap()
    for name, shape in OUT.items():
        aps[name] = nc.dram_tensor(f"out_{name}", shape, F32, kind="ExternalOutput").ap()
    build(nc, aps, None)
    r = run_bass_kernel_spmd(nc, [arrays], core_ids=[0]).results[0]
    return tuple(r[f"out_{name}"] for name in OUT)
```
